# Optimizing a Trainium2 kernel written in Bass

```python
import jax, jax.numpy as jnp
from jax import lax
import numpy as np
import math
import jax
import jax.numpy as jnp

D_MODEL = 1024
BATCH = 1
SEQ = 512
DEPTH = 2

PLE_DIM = 256
HEAD_DIM = 64
N_Q_HEADS = 16
N_KV_HEADS = 4
Q_PER_KV = N_Q_HEADS // N_KV_HEADS
WINDOW = 128
BLOCK = 128
ROPE_THETA = 10000.0
ATT_Q = N_Q_HEADS * HEAD_DIM
ATT_KV = N_KV_HEADS * HEAD_DIM
RW_HEADS = 16
RW_HEAD = 64
RW_DIM = RW_HEADS * RW_HEAD
DECAY_RANK = 64
ICLR_RANK = 64
GATE_RANK = 160
RW_SHIFT_COLS = 3 * RW_DIM + DECAY_RANK + ICLR_RANK + GATE_RANK
D_IN = ATT_Q + 2 * ATT_KV + RW_SHIFT_COLS + 2 * D_MODEL
FFN_DIM = 2816
CONV_W = 3
NORM_EPS = 1e-6
GN_EPS = 64e-5


def _split(z, sizes):
    out, off = [], 0
    for s in sizes:
        out.append(z[..., off:off + s])
        off += s
    return out

def rmsnorm(x, g):
    xf = x.astype(jnp.float32)
    y = xf * lax.rsqrt(jnp.mean(xf * xf, axis=-1, keepdims=True) + NORM_EPS)
    return (y * g.astype(jnp.float32)).astype(x.dtype)

def rope(t, positions):
    half = HEAD_DIM // 2
    inv_freq = jnp.power(ROPE_THETA, -jnp.arange(half, dtype=jnp.float32) / half)
    ang = positions.astype(jnp.float32)[..., None] * inv_freq
    cos = jnp.cos(ang)[:, :, None, :]
    sin = jnp.sin(ang)[:, :, None, :]
    tf = t.astype(jnp.float32)
    t1, t2 = tf[..., :half], tf[..., half:]
    return jnp.concatenate([t1 * cos - t2 * sin, t2 * cos + t1 * sin], axis=-1).astype(t.dtype)

def sliding_window_attention(q, k, v, sinks):
    B, S = q.shape[0], q.shape[1]
    nb = S // BLOCK
    qb = q.astype(jnp.float32).reshape(B, nb, BLOCK, N_KV_HEADS, Q_PER_KV, HEAD_DIM)

    def kv_blocks(t):
        t = t.astype(jnp.float32)
        prev = jnp.pad(t, ((0, 0), (BLOCK, 0), (0, 0), (0, 0)))[:, :S]
        return jnp.concatenate([prev.reshape(B, nb, BLOCK, N_KV_HEADS, HEAD_DIM),
                                t.reshape(B, nb, BLOCK, N_KV_HEADS, HEAD_DIM)], axis=2)

    kb, vb = kv_blocks(k), kv_blocks(v)
    s = jnp.einsum('bnqhgd,bnkhd->bnhgqk', qb, kb) * (HEAD_DIM ** -0.5)
    qi = jnp.arange(BLOCK)[:, None]
    kj = jnp.arange(2 * BLOCK)[None, :]
    dist = qi + BLOCK - kj
    band = (dist >= 0) & (dist < WINDOW)
    kpos = jnp.arange(nb)[:, None, None] * BLOCK - BLOCK + kj[None]
    mask = band[None] & (kpos >= 0)
    s = jnp.where(mask[None, :, None, None], s, -jnp.inf)
    sink = sinks.astype(jnp.float32).reshape(N_KV_HEADS, Q_PER_KV)[None, None, :, :, None, None]
    m = jnp.maximum(jnp.max(s, axis=-1, keepdims=True), sink)
    pr = jnp.exp(s - m)
    pr = pr / (jnp.sum(pr, axis=-1, keepdims=True) + jnp.exp(sink - m))
    o = jnp.einsum('bnhgqk,bnkhd->bnqhgd', pr, vb)
    return o.reshape(B, S, ATT_Q).astype(q.dtype)

def rwkv7_scan(r, w, k, v, a, b):
    B, S, H, N = r.shape

    def step(state, inp):
        r_t, w_t, k_t, v_t, a_t, b_t = inp
        sa = jnp.einsum('bhvk,bhk->bhv', state, a_t)
        state = (state * w_t[:, :, None, :] + sa[..., None] * b_t[:, :, None, :]
                 + v_t[..., None] * k_t[:, :, None, :])
        return state, jnp.einsum('bhvk,bhk->bhv', state, r_t)

    xs = tuple(jnp.moveaxis(t.astype(jnp.float32), 1, 0) for t in (r, w, k, v, a, b))
    s0 = jnp.zeros((B, H, N, N), jnp.float32)
    _, y = lax.scan(step, s0, xs)
    return jnp.moveaxis(y, 0, 1)

def rwkv7_time_mix(z, mu, w0, w2, a0, a2, g2, k_k, k_a, r_k, gn_w, gn_b):
    B, S = z.shape[0], z.shape[1]
    zs = z + (jnp.pad(z, ((0, 0), (1, 0), (0, 0)))[:, :S] - z) * mu
    r, k, v, wd, ad, gd = _split(zs, (RW_DIM, RW_DIM, RW_DIM, DECAY_RANK, ICLR_RANK, GATE_RANK))
    w = -jax.nn.softplus(-(w0 + jnp.tanh(wd) @ w2)) - 0.5
    decay = jnp.exp(-jnp.exp(w.astype(jnp.float32)))
    iclr = jax.nn.sigmoid(a0 + ad @ a2)
    g = jax.nn.sigmoid(gd) @ g2

    def heads(t):
        return t.astype(jnp.float32).reshape(B, S, RW_HEADS, RW_HEAD)

    kk = heads(k * k_k)
    kk = kk / jnp.maximum(jnp.sqrt(jnp.sum(kk * kk, axis=-1, keepdims=True)), 1e-12)
    k = k * (1.0 + (iclr - 1.0) * k_a)
    rh, kh, vh, ah = heads(r), heads(k), heads(v), heads(iclr)
    y = rwkv7_scan(rh, heads(decay), kh, vh, -kk, kk * ah)
    mean = jnp.mean(y, axis=-1, keepdims=True)
    var = jnp.mean(jnp.square(y - mean), axis=-1, keepdims=True)
    y = ((y - mean) * lax.rsqrt(var + GN_EPS)).reshape(B, S, RW_DIM) * gn_w + gn_b
    bonus = jnp.sum(rh * kh * r_k.astype(jnp.float32), axis=-1, keepdims=True) * vh
    out = (y + bonus.reshape(B, S, RW_DIM)) * g
    return out.astype(z.dtype)

def causal_dwconv(u, w, b):
    C = u.shape[-1]
    y = lax.conv_general_dilated(u, w[:, None, :].astype(u.dtype), window_strides=(1,),
                                 padding=[(CONV_W - 1, 0)],
                                 dimension_numbers=('NWC', 'WIO', 'NWC'),
                                 feature_group_count=C)
    return y + b

def hybrid_layer(x, p_i, positions, norm_mix_pre, w_in, att_sinks, w_o_att, rw_mu, rw_w0,
                 rw_w2, rw_a0, rw_a2, rw_g2, rw_k_k, rw_k_a, rw_r_k, rw_gn_w, rw_gn_b,
                 w_o_rw, w_out, norm_mix_post, norm_ffn_pre, w_up, conv_w, conv_b, w_down,
                 norm_ffn_post, w_ple, w_ple_gate, norm_ple):
    B, S = x.shape[0], x.shape[1]
    h = rmsnorm(x, norm_mix_pre)
    proj = h @ w_in
    q, k, v, rw, gate_a, gate_b = _split(proj, (ATT_Q, ATT_KV, ATT_KV, RW_SHIFT_COLS, D_MODEL, D_MODEL))
    q = rope(q.reshape(B, S, N_Q_HEADS, HEAD_DIM), positions)
    k = rope(k.reshape(B, S, N_KV_HEADS, HEAD_DIM), positions)
    v = v.reshape(B, S, N_KV_HEADS, HEAD_DIM)
    y_att = sliding_window_attention(q, k, v, att_sinks) @ w_o_att
    y_rw = rwkv7_time_mix(rw, rw_mu, rw_w0, rw_w2, rw_a0, rw_a2, rw_g2, rw_k_k, rw_k_a,
                          rw_r_k, rw_gn_w, rw_gn_b) @ w_o_rw
    mixed = jax.nn.sigmoid(gate_a) * y_att + jax.nn.sigmoid(gate_b) * y_rw
    x = x + rmsnorm(mixed @ w_out, norm_mix_post)
    h = rmsnorm(x, norm_ffn_pre)
    u = causal_dwconv(h @ w_up, conv_w, conv_b)
    ua, ub = _split(u, (FFN_DIM, FFN_DIM))
    x = x + rmsnorm((jax.nn.gelu(ua) * ub) @ w_down, norm_ffn_post)
    e = p_i @ w_ple
    gate = jax.nn.sigmoid(x @ w_ple_gate)
    x = x + rmsnorm(gate * e, norm_ple)
    return x

def first_inputs(seed: int = 0) -> dict:
    key = jax.random.key(seed)
    ks = iter(jax.random.split(key, 40))

    def nrm(shape, scale):
        return jax.random.normal(next(ks), shape, jnp.float32) * scale

    def gain(n):
        return 1.0 + nrm((DEPTH, n), 0.05)

    L = DEPTH
    return {
        'x': nrm((BATCH, SEQ, D_MODEL), 1.0),
        'p': nrm((DEPTH, BATCH, SEQ, PLE_DIM), 1.0),
        'positions': jnp.broadcast_to(jnp.arange(SEQ, dtype=jnp.int32)[None], (BATCH, SEQ)),
        'norm_mix_pre': gain(D_MODEL),
        'w_in': nrm((L, D_MODEL, D_IN), D_MODEL ** -0.5),
        'att_sinks': nrm((L, N_Q_HEADS), 0.5),
        'w_o_att': nrm((L, ATT_Q, D_MODEL), ATT_Q ** -0.5),
        'rw_mu': jax.random.uniform(next(ks), (L, RW_SHIFT_COLS), jnp.float32),
        'rw_w0': nrm((L, RW_DIM), 0.5),
        'rw_w2': nrm((L, DECAY_RANK, RW_DIM), DECAY_RANK ** -0.5),
        'rw_a0': nrm((L, RW_DIM), 0.5),
        'rw_a2': nrm((L, ICLR_RANK, RW_DIM), ICLR_RANK ** -0.5),
        'rw_g2': nrm((L, GATE_RANK, RW_DIM), GATE_RANK ** -0.5),
        'rw_k_k': 0.85 + nrm((L, RW_DIM), 0.1),
        'rw_k_a': 1.0 + nrm((L, RW_DIM), 0.1),
        'rw_r_k': nrm((L, RW_HEADS, RW_HEAD), 0.1),
        'rw_gn_w': gain(RW_DIM),
        'rw_gn_b': nrm((L, RW_DIM), 0.01),
        'w_o_rw': nrm((L, RW_DIM, D_MODEL), RW_DIM ** -0.5),
        'w_out': nrm((L, D_MODEL, D_MODEL), D_MODEL ** -0.5),
        'norm_mix_post': gain(D_MODEL),
        'norm_ffn_pre': gain(D_MODEL),
        'w_up': nrm((L, D_MODEL, 2 * FFN_DIM), D_MODEL ** -0.5),
        'conv_w': nrm((L, CONV_W, 2 * FFN_DIM), CONV_W ** -0.5),
        'conv_b': nrm((L, 2 * FFN_DIM), 0.01),
        'w_down': nrm((L, FFN_DIM, D_MODEL), FFN_DIM ** -0.5),
        'norm_ffn_post': gain(D_MODEL),
        'w_ple': nrm((L, PLE_DIM, D_MODEL), PLE_DIM ** -0.5),
        'w_ple_gate': nrm((L, D_MODEL, D_MODEL), D_MODEL ** -0.5),
        'norm_ple': gain(D_MODEL),
    }

def first_block(x, p, positions, norm_mix_pre, w_in, att_sinks, w_o_att, rw_mu, rw_w0, rw_w2,
              rw_a0, rw_a2, rw_g2, rw_k_k, rw_k_a, rw_r_k, rw_gn_w, rw_gn_b, w_o_rw, w_out,
              norm_mix_post, norm_ffn_pre, w_up, conv_w, conv_b, w_down, norm_ffn_post,
              w_ple, w_ple_gate, norm_ple):
    for i in range(DEPTH):
        x = hybrid_layer(x, p[i], positions, norm_mix_pre[i], w_in[i], att_sinks[i], w_o_att[i],
                         rw_mu[i], rw_w0[i], rw_w2[i], rw_a0[i], rw_a2[i], rw_g2[i], rw_k_k[i],
                         rw_k_a[i], rw_r_k[i], rw_gn_w[i], rw_gn_b[i], w_o_rw[i], w_out[i],
                         norm_mix_post[i], norm_ffn_pre[i], w_up[i], conv_w[i], conv_b[i],
                         w_down[i], norm_ffn_post[i], w_ple[i], w_ple_gate[i], norm_ple[i])
    return x


GRID_W = 64
CTX_LEN = 256
N_MIXERS = 3
Q_BLOCK = 128
ROPE_BASE = 10000.0

DIFF_DH = 64
DIFF_HEADS = D_MODEL // (2 * DIFF_DH)
GQA_DH = 128
GQA_HEADS = D_MODEL // GQA_DH
GQA_KV_HEADS = max(GQA_HEADS // 4, 1)
GQA_GROUP = GQA_HEADS // GQA_KV_HEADS
GLA_HEADS = 4
GLA_DK = D_MODEL // 2
GLA_DV = D_MODEL
GLA_DK_H = GLA_DK // GLA_HEADS
GLA_DV_H = GLA_DV // GLA_HEADS
GLA_GATE_RANK = 16
GLA_TAU = 16.0
GLA_CHUNK = 64
FFN_HIDDEN = ((8 * D_MODEL // 3 + 255) // 256) * 256

N_A = len(range(0, DEPTH, N_MIXERS))
N_B = len(range(1, DEPTH, N_MIXERS))
N_C = len(range(2, DEPTH, N_MIXERS))


def rmsnorm_2(x, g):
    x32 = x.astype(jnp.float32)
    y = x32 * lax.rsqrt(jnp.mean(x32 * x32, axis=-1, keepdims=True) + NORM_EPS)
    return (y * g.astype(jnp.float32)).astype(x.dtype)

def modulate(t, shift, scale):
    return t * (1 + scale) + shift

def swiglu(t, w_gu, w_down):
    gate, up = jnp.split(t @ w_gu, 2, axis=-1)
    return (jax.nn.silu(gate) * up) @ w_down

def axial_rope_tables(n_tokens, head_dim):
    rows = n_tokens // GRID_W
    row = jnp.broadcast_to(jnp.arange(rows)[:, None], (rows, GRID_W)).reshape(-1)
    col = jnp.broadcast_to(jnp.arange(GRID_W)[None, :], (rows, GRID_W)).reshape(-1)
    half = head_dim // 2
    inv = ROPE_BASE ** (-jnp.arange(0, half, 2, dtype=jnp.float32) / half)

    def axis_angles(pos):
        a = pos.astype(jnp.float32)[:, None] * inv[None, :]
        return jnp.concatenate([a, a], axis=-1)

    ang = jnp.concatenate([axis_angles(row), axis_angles(col)], axis=-1)
    return jnp.cos(ang), jnp.sin(ang)

def apply_axial_rope(x, cos, sin):
    q = x.shape[-1] // 4
    x32 = x.astype(jnp.float32)
    xr = x32.reshape(*x.shape[:-1], 2, 2, q)
    rot = jnp.stack([-xr[..., 1, :], xr[..., 0, :]], axis=-2).reshape(x.shape)
    return (x32 * cos + rot * sin).astype(x.dtype)

def sweep_query_blocks(fn, q):
    B, H, L, d = q.shape
    nb = L // Q_BLOCK
    qb = q.reshape(B, H, nb, Q_BLOCK, d).transpose(2, 0, 1, 3, 4)
    out = lax.map(fn, qb)
    return out.transpose(1, 2, 0, 3, 4).reshape(B, out.shape[2], L, out.shape[-1])

def diff_attention(h, hc, w_in, w_out, q_norm, k_norm, lq1, lk1, lq2, lk2, subln, lambda_init, ctx_out):
    f32 = jnp.float32
    L = h.shape[1]

    def project(t):
        Bt, Lt, _ = t.shape
        q, k, v = jnp.split(t @ w_in, 3, axis=-1)
        q = rmsnorm_2(q.reshape(Bt, Lt, 2 * DIFF_HEADS, DIFF_DH), q_norm).transpose(0, 2, 1, 3)
        k = rmsnorm_2(k.reshape(Bt, Lt, 2 * DIFF_HEADS, DIFF_DH), k_norm).transpose(0, 2, 1, 3)
        v = v.reshape(Bt, Lt, DIFF_HEADS, 2 * DIFF_DH).transpose(0, 2, 1, 3)
        return q, k, v

    q, k, v = project(h)
    qc, kc, vc = project(hc)
    cos, sin = axial_rope_tables(L, DIFF_DH)
    q = apply_axial_rope(q, cos, sin)
    k = apply_axial_rope(k, cos, sin)
    lam = (jnp.exp(jnp.sum(lq1.astype(f32) * lk1.astype(f32)))
           - jnp.exp(jnp.sum(lq2.astype(f32) * lk2.astype(f32))) + lambda_init)

    def pair(t):
        return t.reshape(t.shape[0], DIFF_HEADS, 2, t.shape[2], t.shape[3])

    def attend(qb, keys, vals):
        s = jnp.einsum('bhmtd,bhmsd->bhmts', pair(qb), keys).astype(f32) * DIFF_DH ** -0.5
        p = jax.nn.softmax(s, axis=-1)
        a = (p[:, :, 0] - lam * p[:, :, 1]).astype(vals.dtype)
        return jnp.einsum('bhts,bhse->bhte', a, vals)

    def finish(o):
        Bt, _, Lt, _ = o.shape
        o = rmsnorm_2(o, subln) * (1.0 - lambda_init)
        return o.transpose(0, 2, 1, 3).reshape(Bt, Lt, DIFF_HEADS * 2 * DIFF_DH) @ w_out

    keys = pair(jnp.concatenate([kc, k], axis=2))
    vals = jnp.concatenate([vc, v], axis=2)
    y = finish(sweep_query_blocks(lambda qb: attend(qb, keys, vals), q))
    yc = finish(attend(qc, pair(kc), vc)) if ctx_out else None
    return y, yc

def gqa_attention(h, hc, w_in, w_out, q_norm, k_norm, ctx_out):
    f32 = jnp.float32
    L = h.shape[1]
    kv_w = GQA_KV_HEADS * GQA_DH

    def project(t):
        Bt, Lt, _ = t.shape
        q, k, v = jnp.split(t @ w_in, [GQA_HEADS * GQA_DH, GQA_HEADS * GQA_DH + kv_w], axis=-1)
        q = rmsnorm_2(q.reshape(Bt, Lt, GQA_HEADS, GQA_DH), q_norm).transpose(0, 2, 1, 3)
        k = rmsnorm_2(k.reshape(Bt, Lt, GQA_KV_HEADS, GQA_DH), k_norm).transpose(0, 2, 1, 3)
        v = v.reshape(Bt, Lt, GQA_KV_HEADS, GQA_DH).transpose(0, 2, 1, 3)
        return q, k, v

    q, k, v = project(h)
    qc, kc, vc = project(hc)
    cos, sin = axial_rope_tables(L, GQA_DH)
    q = apply_axial_rope(q, cos, sin)
    k = apply_axial_rope(k, cos, sin)

    def attend(qb, keys, vals):
        Bq, _, T, _ = qb.shape
        qg = qb.reshape(Bq, GQA_KV_HEADS, GQA_GROUP, T, GQA_DH)
        s = jnp.einsum('bkgtd,bksd->bkgts', qg, keys).astype(f32) * GQA_DH ** -0.5
        p = jax.nn.softmax(s, axis=-1).astype(vals.dtype)
        o = jnp.einsum('bkgts,bksd->bkgtd', p, vals)
        return o.reshape(Bq, GQA_HEADS, T, GQA_DH)

    def finish(o):
        Bt, _, Lt, _ = o.shape
        return o.transpose(0, 2, 1, 3).reshape(Bt, Lt, GQA_HEADS * GQA_DH) @ w_out

    keys = jnp.concatenate([kc, k], axis=2)
    vals = jnp.concatenate([vc, v], axis=2)
    y = finish(sweep_query_blocks(lambda qb: attend(qb, keys, vals), q))
    yc = finish(attend(qc, kc, vc)) if ctx_out else None
    return y, yc

def gla_chunk_scan(q, k, v, g, s0):
    f32 = jnp.float32
    B, H, L, _ = q.shape
    n = L // GLA_CHUNK
    mask = jnp.tril(jnp.ones((GLA_CHUNK, GLA_CHUNK), dtype=bool))[:, :, None]

    def to_chunks(t):
        return t.reshape(B, H, n, GLA_CHUNK, t.shape[-1]).transpose(2, 0, 1, 3, 4)

    def step(S, inp):
        qc, kc, vc, gc = inp
        qf, kf, vf = qc.astype(f32), kc.astype(f32), vc.astype(f32)
        b = jnp.cumsum(gc.astype(f32), axis=-2)
        o_inter = jnp.einsum('bhtk,bhkv->bhtv', qf * jnp.exp(b), S)
        rel = jnp.where(mask, b[:, :, :, None, :] - b[:, :, None, :, :], -jnp.inf)
        A = jnp.einsum('bhtk,bhtsk,bhsk->bhts', qf, jnp.exp(rel), kf)
        o = o_inter + jnp.einsum('bhts,bhsv->bhtv', A, vf)
        b_last = b[:, :, -1, :]
        S = jnp.exp(b_last)[..., None] * S + jnp.einsum(
            'bhsk,bhsv->bhkv', kf * jnp.exp(b_last[:, :, None, :] - b), vf)
        return S, o.astype(v.dtype)

    S, o = lax.scan(step, s0, (to_chunks(q), to_chunks(k), to_chunks(v), to_chunks(g)))
    o = o.transpose(1, 2, 0, 3, 4).reshape(B, H, L, v.shape[-1])
    return o, S

def gla_mixer(h, hc, w_in, gw1_f, gw2_f, gb_f, gw1_b, gw2_b, gb_b, out_norm, w_out, ctx_out):
    B = h.shape[0]

    def project(t):
        Bt, Lt, _ = t.shape
        q, k, v, r = jnp.split(t @ w_in, [GLA_DK, 2 * GLA_DK, 2 * GLA_DK + GLA_DV], axis=-1)

        def heads(z, e):
            return z.reshape(Bt, Lt, GLA_HEADS, e).transpose(0, 2, 1, 3)

        def log_decay(w1, w2, b):
            return heads(jax.nn.log_sigmoid(((t @ w1) @ w2 + b).astype(jnp.float32)) / GLA_TAU, GLA_DK_H)

        return (heads(q, GLA_DK_H) * GLA_DK_H ** -0.5, heads(k, GLA_DK_H), heads(v, GLA_DV_H), r,
                log_decay(gw1_f, gw2_f, gb_f), log_decay(gw1_b, gw2_b, gb_b))

    def flip(z):
        return jnp.flip(z, axis=2)

    q, k, v, r, g_f, g_b = project(h)
    qc, kc, vc, rc, gc_f, gc_b = project(hc)
    zeros = jnp.zeros((B, GLA_HEADS, GLA_DK_H, GLA_DV_H), jnp.float32)
    oc_f, sc_f = gla_chunk_scan(qc, kc, vc, gc_f, zeros)
    oc_b, sc_b = gla_chunk_scan(flip(qc), flip(kc), flip(vc), flip(gc_b), zeros)
    o_f, _ = gla_chunk_scan(q, k, v, g_f, sc_f)
    o_b, _ = gla_chunk_scan(flip(q), flip(k), flip(v), flip(g_b), sc_b)

    def finish(o, gate_in):
        Bt, _, Lt, _ = o.shape
        o = rmsnorm_2(o, out_norm).transpose(0, 2, 1, 3).reshape(Bt, Lt, GLA_DV)
        return (o * jax.nn.silu(gate_in)) @ w_out

    y = finish(o_f + flip(o_b), r)
    yc = finish(oc_f + flip(oc_b), rc) if ctx_out else None
    return y, yc

def second_inputs(seed: int = 0) -> dict:
    key = jax.random.key(seed)
    ks = jax.random.split(key, 32)
    f32 = jnp.float32
    D = D_MODEL

    def nrm(k, shape, scale):
        return scale * jax.random.normal(k, shape, f32)

    def gain(k, shape):
        return 1.0 + 0.02 * jax.random.normal(k, shape, f32)

    return {
        'x': nrm(ks[0], (BATCH, SEQ, D), 1.0),
        'c': nrm(ks[1], (BATCH, D), 1.0),
        'ctx': nrm(ks[2], (BATCH, CTX_LEN, D), 1.0),
        'c_ctx': nrm(ks[3], (D,), 1.0),
        'ada_w': nrm(ks[4], (DEPTH, D, 6 * D), 0.5 * D ** -0.5),
        'ada_b': nrm(ks[5], (DEPTH, 6 * D), 0.01),
        'norm1_g': gain(ks[6], (DEPTH, D)),
        'norm2_g': gain(ks[7], (DEPTH, D)),
        'ffn_w_gu': nrm(ks[8], (DEPTH, D, 2 * FFN_HIDDEN), D ** -0.5),
        'ffn_w_down': nrm(ks[9], (DEPTH, FFN_HIDDEN, D), FFN_HIDDEN ** -0.5),
        'diff_w_in': nrm(ks[10], (N_A, D, 3 * D), D ** -0.5),
        'diff_w_out': nrm(ks[11], (N_A, D, D), D ** -0.5),
        'diff_q_norm': gain(ks[12], (N_A, DIFF_DH)),
        'diff_k_norm': gain(ks[13], (N_A, DIFF_DH)),
        'diff_lambda_q1': nrm(ks[14], (N_A, DIFF_DH), 0.1),
        'diff_lambda_k1': nrm(ks[15], (N_A, DIFF_DH), 0.1),
        'diff_lambda_q2': nrm(ks[16], (N_A, DIFF_DH), 0.1),
        'diff_lambda_k2': nrm(ks[17], (N_A, DIFF_DH), 0.1),
        'diff_subln': gain(ks[18], (N_A, 2 * DIFF_DH)),
        'gqa_w_in': nrm(ks[19], (N_B, D, GQA_HEADS * GQA_DH + 2 * GQA_KV_HEADS * GQA_DH), D ** -0.5),
        'gqa_w_out': nrm(ks[20], (N_B, GQA_HEADS * GQA_DH, D), (GQA_HEADS * GQA_DH) ** -0.5),
        'gqa_q_norm': gain(ks[21], (N_B, GQA_DH)),
        'gqa_k_norm': gain(ks[22], (N_B, GQA_DH)),
        'gla_w_in': nrm(ks[23], (N_C, D, 2 * GLA_DK + 2 * GLA_DV), D ** -0.5),
        'gla_gate_w1_fwd': nrm(ks[24], (N_C, D, GLA_GATE_RANK), D ** -0.5),
        'gla_gate_w2_fwd': nrm(ks[25], (N_C, GLA_GATE_RANK, GLA_DK), GLA_GATE_RANK ** -0.5),
        'gla_gate_b_fwd': nrm(ks[26], (N_C, GLA_DK), 0.01),
        'gla_gate_w1_bwd': nrm(ks[27], (N_C, D, GLA_GATE_RANK), D ** -0.5),
        'gla_gate_w2_bwd': nrm(ks[28], (N_C, GLA_GATE_RANK, GLA_DK), GLA_GATE_RANK ** -0.5),
        'gla_gate_b_bwd': nrm(ks[29], (N_C, GLA_DK), 0.01),
        'gla_out_norm': gain(ks[30], (N_C, GLA_DV_H)),
        'gla_w_out': nrm(ks[31], (N_C, GLA_DV, D), GLA_DV ** -0.5),
    }

def second_block(x, c, ctx, c_ctx, ada_w, ada_b, norm1_g, norm2_g, ffn_w_gu, ffn_w_down,
              diff_w_in, diff_w_out, diff_q_norm, diff_k_norm, diff_lambda_q1, diff_lambda_k1,
              diff_lambda_q2, diff_lambda_k2, diff_subln, gqa_w_in, gqa_w_out, gqa_q_norm, gqa_k_norm,
              gla_w_in, gla_gate_w1_fwd, gla_gate_w2_fwd, gla_gate_b_fwd, gla_gate_w1_bwd,
              gla_gate_w2_bwd, gla_gate_b_bwd, gla_out_norm, gla_w_out):
    xc = ctx
    cond_lat = jax.nn.silu(c)
    cond_ctx = jax.nn.silu(c_ctx)
    for i in range(DEPTH):
        last = i == DEPTH - 1
        mod = (cond_lat @ ada_w[i] + ada_b[i])[:, None, :]
        modc = (cond_ctx @ ada_w[i] + ada_b[i])[None, None, :]
        sh1, sc1, g1, sh2, sc2, g2 = jnp.split(mod, 6, axis=-1)
        csh1, csc1, cg1, csh2, csc2, cg2 = jnp.split(modc, 6, axis=-1)

        h = modulate(rmsnorm_2(x, norm1_g[i]), sh1, sc1)
        hc = modulate(rmsnorm_2(xc, norm1_g[i]), csh1, csc1)
        kind, j = i % N_MIXERS, i // N_MIXERS
        if kind == 0:
            lambda_init = 0.8 - 0.6 * math.exp(-0.3 * i)
            y, yc = diff_attention(h, hc, diff_w_in[j], diff_w_out[j], diff_q_norm[j], diff_k_norm[j],
                                   diff_lambda_q1[j], diff_lambda_k1[j], diff_lambda_q2[j],
                                   diff_lambda_k2[j], diff_subln[j], lambda_init, not last)
        elif kind == 1:
            y, yc = gqa_attention(h, hc, gqa_w_in[j], gqa_w_out[j], gqa_q_norm[j], gqa_k_norm[j], not last)
        else:
            y, yc = gla_mixer(h, hc, gla_w_in[j], gla_gate_w1_fwd[j], gla_gate_w2_fwd[j], gla_gate_b_fwd[j],
                              gla_gate_w1_bwd[j], gla_gate_w2_bwd[j], gla_gate_b_bwd[j],
                              gla_out_norm[j], gla_w_out[j], not last)

        x = x + g1 * y
        x = x + g2 * swiglu(modulate(rmsnorm_2(x, norm2_g[i]), sh2, sc2), ffn_w_gu[i], ffn_w_down[i])
        if not last:
            xc = xc + cg1 * yc
            xc = xc + cg2 * swiglu(modulate(rmsnorm_2(xc, norm2_g[i]), csh2, csc2), ffn_w_gu[i], ffn_w_down[i])
    return x


def setup_inputs(seed=0):
    out = dict(first_inputs(seed))
    for name, value in second_inputs(seed + 1).items():
        if name != "x":
            out[name + "_2"] = value
    return out


def reference(
    x, p, positions, norm_mix_pre, w_in, att_sinks, w_o_att, rw_mu, rw_w0, rw_w2, rw_a0, rw_a2,
    rw_g2, rw_k_k, rw_k_a, rw_r_k, rw_gn_w, rw_gn_b, w_o_rw, w_out, norm_mix_post, norm_ffn_pre,
    w_up, conv_w, conv_b, w_down, norm_ffn_post, w_ple, w_ple_gate, norm_ple, c_2, ctx_2,
    c_ctx_2, ada_w_2, ada_b_2, norm1_g_2, norm2_g_2, ffn_w_gu_2, ffn_w_down_2, diff_w_in_2,
    diff_w_out_2, diff_q_norm_2, diff_k_norm_2, diff_lambda_q1_2, diff_lambda_k1_2,
    diff_lambda_q2_2, diff_lambda_k2_2, diff_subln_2, gqa_w_in_2, gqa_w_out_2, gqa_q_norm_2,
    gqa_k_norm_2, gla_w_in_2, gla_gate_w1_fwd_2, gla_gate_w2_fwd_2, gla_gate_b_fwd_2,
    gla_gate_w1_bwd_2, gla_gate_w2_bwd_2, gla_gate_b_bwd_2, gla_out_norm_2, gla_w_out_2,
):
    x = first_block(
        x, p, positions, norm_mix_pre, w_in, att_sinks, w_o_att, rw_mu, rw_w0, rw_w2, rw_a0,
        rw_a2, rw_g2, rw_k_k, rw_k_a, rw_r_k, rw_gn_w, rw_gn_b, w_o_rw, w_out, norm_mix_post,
        norm_ffn_pre, w_up, conv_w, conv_b, w_down, norm_ffn_post, w_ple, w_ple_gate, norm_ple,
    )
    return second_block(
        x, c_2, ctx_2, c_ctx_2, ada_w_2, ada_b_2, norm1_g_2, norm2_g_2, ffn_w_gu_2,
        ffn_w_down_2, diff_w_in_2, diff_w_out_2, diff_q_norm_2, diff_k_norm_2, diff_lambda_q1_2,
        diff_lambda_k1_2, diff_lambda_q2_2, diff_lambda_k2_2, diff_subln_2, gqa_w_in_2,
        gqa_w_out_2, gqa_q_norm_2, gqa_k_norm_2, gla_w_in_2, gla_gate_w1_fwd_2,
        gla_gate_w2_fwd_2, gla_gate_b_fwd_2, gla_gate_w1_bwd_2, gla_gate_w2_bwd_2,
        gla_gate_b_bwd_2, gla_out_norm_2, gla_w_out_2,
    )


_drawn_inputs = setup_inputs


def setup_inputs(seed=0):
    import zlib

    import numpy as np

    out = dict(_drawn_inputs(seed))
    spreads = {}
    factors = {'att_sinks': 4.557,
     'rw_gn_b': 5.147,
     'conv_b': 4.876,
     'ctx_2': 3.694,
     'ada_b_2': 8.0,
     'norm1_g_2': 8.0,
     'norm2_g_2': 8.0,
     'diff_q_norm_2': 8.0,
     'diff_k_norm_2': 8.0,
     'diff_lambda_q1_2': 64.0,
     'diff_lambda_k1_2': 64.0,
     'diff_lambda_q2_2': 8.0,
     'diff_lambda_k2_2': 8.0,
     'diff_subln_2': 8.0,
     'gqa_q_norm_2': 8.0,
     'gqa_k_norm_2': 8.0}
    for name, (base, spread) in spreads.items():
        noise = np.random.default_rng([zlib.crc32(name.encode()), seed]).standard_normal(out[name].shape)
        drawn = base * np.exp(spread * noise) if base else spread * noise
        out[name] = jnp.asarray(drawn.astype(out[name].dtype))
    for name, factor in factors.items():
        out[name] = (out[name] * factor).astype(out[name].dtype)
    return out
```

```python
from contextlib import ExitStack

import numpy as np

import concourse.bass as bass
import concourse.mybir as mybir

F32 = mybir.dt.float32
F32R = mybir.dt.float32r
I32 = mybir.dt.int32
ALU = mybir.AluOpType
ACT = mybir.ActivationFunctionType
AX_X = mybir.AxisListType.X
ET = mybir.EngineType

P = 128
D = 1024
DT = D // P
S = 512
CTX = 256
T2 = S + CTX
L = 2
PLE = 256
FFN = 2816
FT = FFN // P
NQH, NKVH, HD = 16, 4, 64
CH = 64
NCH = S // CH
EPS = 1e-6
GN_EPS = 64e-5
NEG = -1e30
LAM_INIT = 0.8 - 0.6 * float(np.exp(-0.3 * 0))
DECAY_C = float(np.exp(-0.5))

PIECE = 8
SLOTS = 4

N_HYB = 64 + 16 + 16 + 128 + 24 + 192 + 8 + 16 + 128 + 64 + 16 * FT + 8 * FT + 80
TURN = PIECE * SLOTS
PAD_HYB = -N_HYB % TURN
N_DIFF = 384 + 64 + 64 + 64 + 64 + 16 * FT + 8 * FT
N_GQA = 384 + 64 + 16 + 16 + 64 + 16 * FT + 8 * FT
N_TILES = L * (N_HYB + PAD_HYB) + N_DIFF + N_GQA
N_TILES += -N_TILES % TURN

COLS1 = {}
_at = 0
for _n, _w in (("pre", 8), ("mu_rkv", 24), ("mu_low", 3), ("w0", 8), ("a0", 8), ("k_k", 8), ("k_a", 8),
               ("r_k", 8), ("gn_w", 8), ("gn_b", 8), ("post", 8), ("fpre", 8), ("cw", 132), ("cb", 44),
               ("fpost", 8), ("ple", 8), ("sinks", 16)):
    COLS1[_n] = _at
    _at += _w
NC1 = _at
COLS2 = {}
_at = 0
for _n, _w in (("ada_b", 96), ("norm1", 16), ("norm2", 16), ("dq", 1), ("dk", 1), ("gq", 1), ("gk", 1),
               ("subln", 1), ("lam", 4), ("cond", 16)):
    COLS2[_n] = _at
    _at += _w
NC2 = _at

CONST = {}
_at = 0
for _n, _w in (("ident", 128), ("ones_d", 128), ("ones_128", 128), ("blk", 128), ("blk_64", 128),
               ("rot_nx", 128), ("rot_ax64", 128), ("rot_ax128", 128), ("m_diagT", 64), ("m_offT", 64),
               ("m_diag", 64), ("m_incT", 64), ("m_strT", 64), ("eye64", 64), ("segs", 512),
               ("band", 256), ("invf", 1)):
    CONST[_n] = _at
    _at += _w
NCONST = _at


class Loop:
    def __init__(self, name, n, var):
        self.name, self.n, self.var, self.open = name, n, var, True


class Counter:

    def __init__(self, k, name):
        self.k, self.name = k, name
        self.sem = k.nc.alloc_semaphore(name)
        self.const = 0
        k.counters.append(self)

    def now(self):
        return (self, self.const, tuple((lp, self.k.per.get((lp.name, self.name), 0)) for lp in self.k.loops))


class Engine:

    def __init__(self, k, eng, name, chain=True):
        self.k, self.eng, self.name, self.chain = k, eng, name, chain
        self.done = Counter(k, f"{name}_done")
        self.tick = k.nc.alloc_semaphore(f"{name}_tick")
        self.seen = {}

    def wait(self, *marks):
        regs, consts = [], []
        for m in marks:
            if m is None:
                continue
            if isinstance(m, list):
                for x in m:
                    self.wait(x)
                continue
            c, const, coefs = m
            open_ = []
            for lp, per in coefs:
                if lp.open:
                    if per:
                        open_.append((lp, per))
                else:
                    const += per * (lp.n - 1)
            if const <= 0 and not open_:
                continue
            key = (c.name, tuple(lp.name for lp, _ in open_))
            if self.seen.get(key, -1) >= const:
                continue
            self.seen[key] = const
            (regs if open_ else consts).append((c, const, open_))
        for c, const, open_ in regs:
            v = const
            for lp, per in open_:
                v = lp.var * per + v
            self.eng.wait_ge(c.sem, v)
            self.eng.sem_inc(self.tick, 1)
        for c, const, _ in consts:
            self.eng.wait_ge(c.sem, const)

    def do(self, fn, *args, w=(), **kw):
        if self.chain:
            self.wait(self.done.now())
        self.wait(*w) if isinstance(w, (list, tuple)) and not (len(w) == 3 and isinstance(w[0], Counter)) else self.wait(w)
        self.done.const += 1
        fn(*args, **kw).then_inc(self.done.sem, 1)
        return self.done.now()

    def dma(self, counter, dst, src, w=()):
        self.wait(*w) if isinstance(w, (list, tuple)) and not (len(w) == 3 and isinstance(w[0], Counter)) else self.wait(w)
        self.eng.dma_start(dst, src).then_inc(counter.sem, 16)
        counter.const += 16
        return counter.now()


class Kit:
    def __init__(self, nc, per):
        self.nc, self.per = nc, per
        self.counted = {}
        self.counters, self.loops = [], []
        self.pe = Engine(self, nc.tensor, "pe", chain=False)
        self.act = Engine(self, nc.scalar, "act")
        self.dve = Engine(self, nc.vector, "dve")
        self.pool = Engine(self, nc.gpsimd, "pool")
        self.engines = (self.pe, self.act, self.dve, self.pool)

    def fence(self):
        marks = [e.done.now() for e in self.engines]
        for e in self.engines:
            e.wait(*[m for m in marks if m[0] is not e.done or e.chain])

    def note(self, name, mark):
        self.counted[("note", name)] = (mark[0].name, mark[1] - self.start[mark[0].name])

    def before(self, name):
        if ("note", name) not in self.per:
            return None
        c_name, local = self.per[("note", name)]
        c = next(c for c in self.counters if c.name == c_name)
        lp = self.loops[-1]
        const = self.start[c_name] + local - self.per[(lp.name, c_name)]
        assert const > 0
        now = c.now()
        return (c, const, now[2])

    def loop(self, name, n, body, fenced=True):
        start = {c.name: c.const for c in self.counters}
        self.start = start
        with self.nc.Fori(0, n, engines=(ET.PE, ET.Activation, ET.DVE, ET.Pool)) as i:
            lp = Loop(name, n, i)
            self.loops.append(lp)
            for e in self.engines:
                e.seen = {}
            if fenced:
                self.fence()
            body(i)
        self.loops.pop()
        lp.open = False
        for c in self.counters:
            one = c.const - start.get(c.name, 0)
            self.counted[(name, c.name)] = one
            c.const = start.get(c.name, 0) + one * n
        for e in self.engines:
            e.seen = {}
        self.fence()


def program(nc, a, per, probe=None):
    k = Kit(nc, per)
    pe, act, dve, pool = k.pe, k.act, k.dve, k.pool
    V, A, G, T = nc.vector, nc.scalar, nc.gpsimd, nc.tensor

    ring = nc.alloc_sbuf_tensor("ring", [P, TURN, P], F32)
    big = nc.alloc_sbuf_tensor("big", [P, 44160], F32)
    con = nc.alloc_sbuf_tensor("con", [P, NCONST], F32)
    tab = nc.alloc_sbuf_tensor("tab", [P, 2, S], F32)
    par = nc.alloc_sbuf_tensor("par", [P, max(NC1, NC2)], F32)
    sml = nc.alloc_sbuf_tensor("sml", [P, 640], F32)
    ps = nc.alloc_psum_tensor("ps", [P, 8, 512], F32)
    x_spill = nc.dram_tensor("x_spill", [P, DT, S], F32)
    m_spill = nc.dram_tensor("m_spill", [P, DT, S], F32)

    def region(at, *shape):
        n = int(np.prod(shape))
        assert at + n <= 44160, (at, shape)
        v = big[:, at:at + n]
        if len(shape) == 2:
            return v.rearrange("p (a b) -> p a b", b=shape[1])
        if len(shape) == 3:
            return v.rearrange("p (a b c) -> p a b c", b=shape[1], c=shape[2])
        return v

    rounded = {}

    def region_r(at, n, width):
        assert at + n * width <= 44160
        out = []
        for o in range(at, at + n * width, width):
            if (o, width) not in rounded:
                rounded[o, width] = nc.alloc_sbuf_tensor_at(f"rounded{o}_{width}", [P, width], F32R,
                                                            offset=nc.lookup_mloc(big).addr + 4 * o)
            out.append(rounded[o, width][:])
        return out

    X = region(0, DT, T2)

    def c_(name, w=None):
        return con[:, CONST[name]:CONST[name] + (w or 128)]

    def p1(name, j=0, w=1):
        return par[:, COLS1[name] + j:COLS1[name] + j + w]

    def p2(name, j=0, w=1):
        return par[:, COLS2[name] + j:COLS2[name] + j + w]

    full = [Counter(k, f"w_full{s}") for s in range(SLOTS)]
    freed = Counter(k, "w_freed")
    sp_tick = nc.alloc_semaphore("sp_tick")
    n_pieces = N_TILES // PIECE
    for s in range(SLOTS):
        nc.sync.dma_start(ring[:, s * PIECE:(s + 1) * PIECE, :], a["w"][s]).then_inc(full[s].sem, 16)
    with nc.sync.Fori(1, n_pieces // SLOTS) as turn:
        for s in range(SLOTS):
            nc.sync.wait_ge(freed.sem, turn * SLOTS + (s - SLOTS + 2))
            nc.sync.sem_inc(sp_tick, 1)
            nc.sync.dma_start(ring[:, s * PIECE:(s + 1) * PIECE, :],
                              a["w"][bass.ds(turn * SLOTS + s, 1)].rearrange("a p t c -> p (a t) c")
                              ).then_inc(full[s].sem, 16)

    class Stream:
        pos = 0

    def w_tiles(n=1):
        at = Stream.pos % TURN
        first = at % PIECE == 0
        assert at // PIECE == (at + n - 1) // PIECE
        if first:
            full[at // PIECE].const += 16
            pe.wait(full[at // PIECE].now())
        Stream.pos += n
        return ring[:, at:at + n, :].rearrange("p a b -> p (a b)"), first

    def mm(out, lhsT, rhs, start, stop, first=False, w=()):
        pe.wait(*w)
        i = T.matmul(out, lhsT, rhs, start=start, stop=stop, skip_group_check=True)
        if first:
            i.then_inc(freed.sem, 1)
            freed.const += 1

    def mm_last(out, lhsT, rhs, start, stop, w=()):
        return pe.do(T.matmul, out, lhsT, rhs, start=start, stop=stop, skip_group_check=True, w=w)

    class Banks:
        def __init__(self, ids):
            self.ids, self.i = ids, 0
            self.read = {b: [] for b in ids}

        def take(self):
            b = self.ids[self.i % len(self.ids)]
            self.i += 1
            return b

    def spend(pos_pad):
        for _ in range(pos_pad):
            w, first = w_tiles()
            if first:
                mm(ps[:, 7, 0:2], w, c_("ident")[:, 0:2], True, True, first=True)

    def linear(n_out, kt, rhs, segs, evac, banks, ready):
        pe.wait(*ready)
        for n in range(n_out):
            bs = [banks.take() for _ in segs]
            pe.wait(*[banks.read[b] for b in bs])
            for q in range(kt):
                w, first = w_tiles()
                for si, (c0, cw) in enumerate(segs):
                    args = (ps[:, bs[si], 0:cw], w, rhs(q, c0, cw), q == 0, q == kt - 1)
                    if q == kt - 1 and si == len(segs) - 1:
                        assert not (first and si == 0)
                        mark = mm_last(*args)
                    else:
                        mm(*args, first=first and si == 0)
            r = evac(n, bs, mark)
            for b in bs:
                banks.read[b] = r

    class Cut:

        def __init__(self, at):
            n = PIECE * P
            *self.hi, lo0, lo1 = region_r(at, 4, n)
            self.lo = [lo0, lo1]
            self.ready, self.free = [[], []], [[], []]
            self.ahead = None

        def cut(self, piece):
            slot, i = piece % SLOTS, piece % 2
            full[slot].const += 16
            raw = ring[:, slot * PIECE:(slot + 1) * PIECE, :].rearrange("p a b -> p (a b)")
            h = act.do(A.copy, self.hi[i], raw, w=[full[slot].now(), *self.free[i]])
            lo = dve.do(V.tensor_tensor, self.lo[i], raw, self.hi[i].bitcast(F32), ALU.subtract,
                        w=[full[slot].now(), h, *self.free[i]])
            self.ready[i] = [lo]
            self.ahead = piece + 1

        def tiles(self, n, more):
            at = Stream.pos % PIECE
            piece = Stream.pos // PIECE
            i = piece % 2
            first = at == 0
            if first:
                if self.ahead is None or self.ahead <= piece:
                    self.cut(piece)
                pe.wait(*self.ready[i])
                if more:
                    self.cut(piece + 1)
            assert at + n <= PIECE
            Stream.pos += n
            sl = slice(at * P, (at + n) * P)
            return self.hi[i][:, sl], self.lo[i][:, sl], first, (i if at + n == PIECE else None)

        def used(self, i, mark):
            if i is not None:
                self.free[i] = [mark]

    def linear3(n_out, kt, act_hi, act_lo, segs, evac, banks, cut, ready, more_after):
        for n in range(n_out):
            bs = [banks.take() for _ in segs]
            pe.wait(*[banks.read[b] for b in bs])
            for q in range(kt):
                more = more_after or (Stream.pos // PIECE + 1) * PIECE < cut_end[0]
                hi, lo, first, whole = cut.tiles(1, more)
                if n == 0:
                    pe.wait(ready(q))
                todo = [(si, w, x) for w, xs in ((hi, (act_hi, act_lo)), (lo, (act_hi,)))
                        for si in range(len(segs)) for x in xs]
                left = [sum(t[0] == si for t in todo) for si in range(len(segs))]
                for m_, (si, w, x) in enumerate(todo):
                    c0, cw = segs[si]
                    left[si] -= 1
                    args = (ps[:, bs[si], 0:cw], w, x(q, c0, cw), q == 0 and left[si] == 2,
                            q == kt - 1 and left[si] == 0)
                    if m_ == len(todo) - 1 and (q == kt - 1 or whole is not None):
                        mark = mm_last(*args)
                        cut.used(whole, mark)
                    else:
                        mm(*args, first=first and m_ == 0)
            r = evac(n, bs, mark)
            for b in bs:
                banks.read[b] = r

    cut_end = [0]

    def cut_up_to(tiles):
        cut_end[0] = Stream.pos + tiles

    def halves(n, raw, hi, lo, w=(), lo_engine=None):
        marks = []
        for j in range(n):
            h = act.do(A.copy, hi(j), raw(j), w=w)
            marks.append(dve.do(V.tensor_tensor, lo(j), raw(j), hi(j).bitcast(F32), ALU.subtract, w=[h, *w]))
        return marks

    def sum_sq(src, n, segs, ones, bank_of, sq, ready=()):
        marks = [None, None]
        for j in range(n):
            t = act.do(A.activation, sq(j % 2), src(j), ACT.Square, w=[marks[j % 2], *ready])
            for si, (c0, cw) in enumerate(segs):
                pe.wait(t)
                args = (ps[:, bank_of[si], 0:cw], ones, sq(j % 2)[:, c0:c0 + cw], j == 0, j == n - 1)
                if si == len(segs) - 1:
                    marks[j % 2] = mm_last(*args)
                else:
                    mm(*args)
        return marks[(n - 1) % 2]

    def rsqrt(dst, src, eps, w=()):
        t = dve.do(V.tensor_scalar, dst, src, eps, None, ALU.add, w=w)
        t = act.do(A.activation, dst, dst, ACT.Sqrt, w=t)
        return dve.do(V.reciprocal, dst, dst, w=t)

    SEG1 = [(0, S)]
    SEG2 = [(0, S), (S, CTX)]

    load_c = Counter(k, "load_const")
    load_x = Counter(k, "load_x")
    load_p = Counter(k, "load_par")
    load_e = Counter(k, "load_ple")
    st_x, ld_x = Counter(k, "store_x"), Counter(k, "reload_x")
    st_m, ld_m = Counter(k, "store_m"), Counter(k, "reload_m")
    out_d = Counter(k, "store_out")
    dump_d = Counter(k, "dump")
    act.dma(load_c, con[:], a["con"])
    act.dma(load_c, tab[:].bitcast(I32)[:, 0, :], a["pos"])
    act.dma(load_x, X[:, :, 0:S], a["x"])
    act.dma(load_x, X[:, :, S:T2], a["ctx"])
    for e in k.engines:
        e.wait(load_c.now(), load_x.now())

    def dump(name, ap):
        if probe and name in probe:
            k.fence()
            act.dma(dump_d, a["d_" + name], ap)
            act.wait(dump_d.now())
            act.do(A.copy, sml[:, 639:640], sml[:, 638:639])
            k.fence()

    dve.do(V.memset, sml[:, 600:640], 0.0)

    TMP0 = 10240
    ang, nn, r_ = region(TMP0, 1, S)[:, 0, :], region(TMP0 + S, 1, S)[:, 0, :], region(TMP0 + 2 * S, 1, S)[:, 0, :]
    TWO_PI = 6.283185307179586
    C1 = 6.28125
    C2 = float(np.float32(TWO_PI - C1).view(np.int32) >> 12 << 12)
    C2 = float(np.array(int(np.float32(TWO_PI - C1).view(np.int32)) >> 12 << 12, np.int32).view(np.float32))
    C3 = TWO_PI - C1 - C2
    MAGIC = 12582912.0
    dve.do(V.tensor_copy, ang, tab[:].bitcast(I32)[:, 0, :])
    dve.do(V.tensor_scalar, ang, ang, con[:, CONST["invf"]:CONST["invf"] + 1], None, ALU.mult)
    for which, shift in ((1, 0.0), (0, 0.25)):
        dve.do(V.tensor_scalar, nn, ang, 1.0 / TWO_PI, shift, ALU.mult, ALU.add)
        dve.do(V.tensor_scalar, nn, nn, MAGIC, MAGIC, ALU.add, ALU.subtract)
        dve.do(V.scalar_tensor_tensor, r_, nn, -C1, ang, ALU.mult, ALU.add)
        dve.do(V.scalar_tensor_tensor, r_, nn, -C2, r_, ALU.mult, ALU.add)
        dve.do(V.scalar_tensor_tensor, r_, nn, -C3, r_, ALU.mult, ALU.add)
        dve.do(V.tensor_scalar, r_, r_, shift * TWO_PI, None, ALU.add)
        t = dve.do(V.tensor_scalar, r_, r_, 3.14159, -3.14159, ALU.min, ALU.max)
        t = act.do(A.activation, tab[:, which, :], r_, ACT.Sin, w=t)
        dve.wait(t)
    COS, SIN = tab[:, 0, :], tab[:, 1, :]
    dump("tab", tab[:])

    def norm_to(dst, segs, gain, bank_of, tmp_at, shift=None):
        lo, wd = 0, sum(c for _, c in segs)
        sq = lambda i: region(tmp_at + i * wd, 1, wd)[:, 0, :]
        rs = region(tmp_at + 2 * wd, 1, wd)[:, 0, :]
        t = sum_sq(lambda j: X[:, j, 0:wd], DT, segs, c_("ones_d"), bank_of, sq)
        for si, (c0, cw) in enumerate(segs):
            rsqrt(rs[:, c0:c0 + cw], ps[:, bank_of[si], 0:cw], EPS, w=t)
        for j in range(DT):
            for si, (c0, cw) in enumerate(segs):
                dve.do(V.scalar_tensor_tensor, dst[:, j, c0:c0 + cw], X[:, j, c0:c0 + cw], gain(j, si),
                       rs[:, c0:c0 + cw], ALU.mult, ALU.mult)
                if shift is not None:
                    dve.do(V.tensor_scalar, dst[:, j, c0:c0 + cw], dst[:, j, c0:c0 + cw], shift(j, si), None, ALU.add)

    def add_normed(Z, gain, bank, tmp_at, ready=()):
        sq = lambda i: region(tmp_at + i * S, 1, S)[:, 0, :]
        rs = sq(2)
        t = sum_sq(lambda j: Z[:, j, :], DT, SEG1, c_("ones_d"), [bank], sq, ready)
        rsqrt(rs, ps[:, bank, :], EPS, w=t)
        for j in range(DT):
            t = dve.do(V.scalar_tensor_tensor, Z[:, j, :], Z[:, j, :], gain(j), rs, ALU.mult, ALU.mult)
            t = pool.do(G.tensor_tensor, X[:, j, 0:S], X[:, j, 0:S], Z[:, j, :], ALU.add, w=t)
        return t

    def ffn_out(A_, Z, segs, banks):
        last = []

        def evac(n, bs, mark):
            r = []
            for si, (c0, cw) in enumerate(segs):
                r.append(act.do(A.copy, Z[:, n, c0:c0 + cw], ps[:, bs[si], 0:cw], w=mark))
            last[:] = r
            return r
        linear(DT, FT, lambda q, c0, cw: A_[:, q, c0:c0 + cw], segs, evac, banks, ())
        return last

    A1 = 10240
    H = region(6144, DT, S)
    TMP = A1 + 20480

    def hybrid(layer):
        act.dma(load_p, par[:, 0:NC1], a["par1"][bass.ds(layer, 1)].rearrange("a p c -> p (a c)"))
        for e in k.engines:
            e.wait(load_p.now())
        norm_to(H, SEG1, lambda j, si: p1("pre", j), [7], TMP)
        dump("h", H)
        k.fence()
        act.dma(st_x, x_spill.ap(), X[:, :, 0:S])
        hr = lambda q, c0, cw: H[:, q, c0:c0 + cw]

        Q, O, KK, VT = (region(A1, DT, S), region(A1 + 4096, DT, S), region(A1 + 8192, 2, S),
                        region(A1 + 9216, 4, 256))
        M = region(A1 + 12288, DT, S)
        banks = Banks([0, 1, 2, 3])
        rot_read = {4: [], 5: []}
        raw = [region(TMP + i * S, 1, S)[:, 0, :] for i in range(2)]
        t1 = [region(TMP + (2 + i) * S, 1, S)[:, 0, :] for i in range(2)]
        t2 = [region(TMP + (4 + i) * S, 1, S)[:, 0, :] for i in range(2)]
        done = {"raw": [[], []], "t1": [[], []]}

        def rope_to(dst):
            def evac(n, bs, mark):
                i = n % 2
                r = act.do(A.copy, raw[i], ps[:, bs[0], :], w=[mark, *done["raw"][i]])
                m = mm_last(ps[:, 4 + i, :], c_("rot_nx"), raw[i], True, True, w=[r, *rot_read[4 + i]])
                c = pool.do(G.tensor_tensor, t1[i], raw[i], COS, ALU.mult, w=[r, *done["t1"][i]])
                s = dve.do(V.tensor_tensor, t2[i], ps[:, 4 + i, :], SIN, ALU.mult, w=m)
                rot_read[4 + i] = [s]
                f = dve.do(V.tensor_tensor, dst[:, n, :], t1[i], t2[i], ALU.add, w=c)
                done["t1"][i] = [f]
                done["raw"][i] = [c, m]
                return [r]
            return evac
        linear(DT, DT, hr, SEG1, rope_to(Q), banks, [dve.done.now()])
        linear(2, DT, hr, SEG1, rope_to(KK), banks, ())
        pe.wait(*[banks.read[b] for b in banks.ids])
        for q in range(DT):
            w, first = w_tiles(2)
            for tt in range(4):
                args = (ps[:, tt, 0:256], H[:, q, tt * P:(tt + 1) * P], w, q == 0, q == DT - 1)
                if q == DT - 1:
                    m = mm_last(*args)
                else:
                    mm(*args, first=first and tt == 0)
        t = act.do(A.copy, VT, ps[:, 0:4, 0:256], w=m)
        dump("q", Q)
        k.fence()

        sc_read, pt_read = [], []
        Pb = [region(TMP + 1024 * (1 + i), 4, 256) for i in range(2)]
        PT = [region(TMP + 1024 * (3 + i), 4, 256) for i in range(2)]
        pt_used = [[], []]
        o_read = {6: [], 7: []}
        pb_used = [[], []]

        def scores(n, g):
            k0 = max(n - 1, 0) * P
            kw = (n + 1) * P - k0
            pe.wait(*sc_read)
            for hh in range(4):
                h = 4 * g + hh
                kr = 64 * (g % 2)
                qs = Q[64 * (h % 2):64 * (h % 2) + 64, h // 2, n * P:(n + 1) * P]
                ks = KD[h % 2][64 * (h % 2):64 * (h % 2) + 64, g, k0:k0 + kw]
                o = ps[:, hh % 2, (hh // 2) * 256 + 256 - kw:(hh // 2) * 256 + 256]
                if hh == 3:
                    return mm_last(o, qs, ks, True, True)
                mm(o, qs, ks, True, True)

        KDUP = region(TMP + 5120, 4, S)
        KD = (KDUP, KDUP)
        for g in range(4):
            src = KK[64 * (g % 2):64 * (g % 2) + 64, g // 2, :]
            for half in range(2):
                act.do(A.copy, KDUP[64 * half:64 * half + 64, g, :], src)
        k.fence()
        steps = [(n, g) for n in range(4) for g in range(4)]
        ready = {}
        Sb2 = [region(TMP + 7168 + 1024 * i, 4, 256) for i in range(2)]

        def span(n):
            kw = P if n == 0 else 256
            return kw, 256 - kw

        def softmax(it):
            n, g = steps[it]
            i = it % 2
            kw, lo = span(n)
            Sb = Sb2[i]
            mx, nm, sm, es = (sml[:, 16 * i + 4 * q:16 * i + 4 * q + 4] for q in range(4))
            band = con[:, CONST["band"] + lo:CONST["band"] + 256].unsqueeze(1).to_broadcast([P, 2, kw])
            for half in range(2):
                t = dve.do(V.tensor_tensor, Sb[:, 2 * half:2 * half + 2, lo:256],
                           ps[:, half, :].rearrange("p (h c) -> p h c", c=256)[:, :, lo:256], band, ALU.add,
                           w=[sc_mark[it], *s_used[i]])
            sc_read[:] = [t]
            dve.do(V.tensor_reduce, mx, Sb[:, :, lo:256], AX_X, ALU.max)
            sink = p1("sinks", 4 * g, 4)
            dve.do(V.scalar_tensor_tensor, mx, mx, HD ** -0.5, sink, ALU.mult, ALU.max)
            dve.do(V.tensor_scalar, nm, mx, -1.0, None, ALU.mult)
            t = dve.do(V.tensor_tensor, es, sink, mx, ALU.subtract)
            for hh in range(4):
                act.do(A.activation, Pb[i][:, hh, lo:256], Sb[:, hh, lo:256], ACT.Exp, bias=nm[:, hh:hh + 1],
                       scale=HD ** -0.5, accum_out=sm[:, hh:hh + 1], w=[t, *pb_used[i]])
            t = act.do(A.activation, es, es, ACT.Exp)
            s_used[i] = [t]
            return t

        def weigh(it, t):
            n, g = steps[it]
            i = it % 2
            kw, lo = span(n)
            sm, es = sml[:, 16 * i + 8:16 * i + 12], sml[:, 16 * i + 12:16 * i + 16]
            dve.do(V.tensor_tensor, sm, sm, es, ALU.add, w=t)
            t = dve.do(V.reciprocal, sm, sm)
            return pool.do(G.tensor_tensor, Pb[i][:, :, lo:256], Pb[i][:, :, lo:256],
                           sm.unsqueeze(2).to_broadcast([P, 4, kw]), ALU.mult, w=t)

        def turn(it):
            n, g = steps[it]
            i = it % 2
            kw, lo = span(n)
            pe.wait(ready[it], *pt_read)
            for hh in range(4):
                for b in range(kw // P):
                    o = ps[:, 2 + hh // 2, (hh % 2) * 256 + b * P:(hh % 2) * 256 + (b + 1) * P]
                    tp = Pb[i][:, hh, lo + b * P:lo + (b + 1) * P]
                    if hh == 3 and b == kw // P - 1:
                        m = pe.do(T.transpose, o, tp, c_("ident"))
                    else:
                        T.transpose(o, tp, c_("ident"))
            pb_used[i] = [m]
            r = []
            for half in range(2):
                e = act if half else dve
                f = A.copy if half else V.tensor_copy
                r.append(e.do(f, PT[i][:, 2 * half:2 * half + 2, 0:kw],
                              ps[:, 2 + half, :].rearrange("p (h c) -> p h c", c=256)[:, :, 0:kw],
                              w=[m, *pt_used[i]]))
            pt_read[:] = r

        def weighted_values(it):
            n, g = steps[it]
            i = it % 2
            kw, lo = span(n)
            bank = 6 + i
            pe.wait(*pt_read, *o_read[bank])
            for hh in range(4):
                half = hh % 2
                for b in range(kw // P):
                    vt = VT[:, (n if n == 0 else n - 1) + b, g * 64:(g + 1) * 64]
                    o = ps[64 * half:64 * half + 64, bank, (hh // 2) * P:(hh // 2 + 1) * P]
                    args = (o, vt, PT[i][:, 2 * (hh % 2) + hh // 2, b * P:(b + 1) * P], b == 0, b == kw // P - 1)
                    if hh == 3 and b == kw // P - 1:
                        m = mm_last(*args)
                    else:
                        mm(*args)
            pt_used[i] = [m]
            o_read[bank] = [act.do(A.copy, O[:, 2 * g:2 * g + 2, n * P:(n + 1) * P],
                                   ps[:, bank, 0:256].rearrange("p (a c) -> p a c", c=P), w=m)]

        sc_mark = {0: scores(*steps[0])}
        s_used = [[], []]
        for it in range(len(steps) + 1):
            if it < len(steps):
                t = softmax(it)
                if it + 1 < len(steps):
                    sc_mark[it + 1] = scores(*steps[it + 1])
            if it > 0:
                turn(it - 1)
            if it < len(steps):
                ready[it] = weigh(it, t)
            if it > 0:
                weighted_values(it - 1)
        dump("o", O)
        k.fence()

        gt = [region(TMP + i * S, 1, S)[:, 0, :] for i in range(2)]

        def gated(src, dst, extra=None):
            banks = Banks([0, 1, 2, 3])
            used = [[], []]
            for n in range(DT):
                i = n % 2

                def ev_gate(_, bs, mark):
                    return [act.do(A.activation, gt[i], ps[:, bs[0], :], ACT.Sigmoid, w=[mark, *used[i]])]

                def ev_y(_, bs, mark):
                    r = dve.do(V.tensor_tensor, dst[:, n, :] if extra is None else gt[i], ps[:, bs[0], :], gt[i],
                               ALU.mult, w=[mark, act.done.now()])
                    used[i] = [r]
                    if extra is not None:
                        used[i] = [dve.do(V.tensor_tensor, dst[:, n, :], gt[i], extra[:, n, :], ALU.add)]
                    return [r]
                linear(1, DT, hr, SEG1, ev_gate, banks, ())
                linear(1, DT, lambda q, c0, cw: src[:, q, c0:c0 + cw], SEG1, ev_y, banks, ())
        gated(O, M)
        dump("m", M)
        k.fence()
        act.dma(st_m, m_spill.ap(), M)

        LOW = region(A1 + 32256, 3, S)
        RKV = region(A1, 3 * DT, S)
        zb = [region(TMP + i * 520, 1, 520)[:, 0, :] for i in range(2)]
        dd = [region(TMP + 1040 + i * S, 1, S)[:, 0, :] for i in range(2)]
        for i in range(2):
            t = dve.do(V.memset, zb[i][:, 0:1], 0.0)
        act.wait(t)

        def shifted(dst, mu):
            used = [[], []]

            def evac(n, bs, mark):
                i = n % 2
                r = act.do(A.copy, zb[i][:, 1:S + 1], ps[:, bs[0], :], w=[mark, *used[i]])
                d = pool.do(G.tensor_tensor, dd[i], zb[i][:, 0:S], zb[i][:, 1:S + 1], ALU.subtract, w=[r, *used[i]])
                u = dve.do(V.scalar_tensor_tensor, dst(n), dd[i], mu(n), zb[i][:, 1:S + 1],
                           ALU.mult, ALU.add, w=d)
                used[i] = [u]
                return [r]
            return evac
        banks = Banks([0, 1, 2, 3])
        linear(3, DT, hr, SEG1, shifted(lambda n: LOW[:, n, :], lambda n: p1("mu_low", n)), banks, ())
        spend_to_turn()
        for e in k.engines:
            e.wait(st_m.now(), st_x.now())

        def rkv(i):
            b = Banks([0, 1, 2, 3])
            linear(DT, DT, hr, SEG1,
                   shifted(lambda n: RKV[:, bass.ds(i * DT + n, 1), :].rearrange("p a c -> p (a c)"),
                           lambda n: par[:, bass.ds(i * DT + (COLS1["mu_rkv"] + n), 1)]), b, ())
        k.loop("rkv", 3, rkv)
        dump("rkv", RKV)
        act.do(A.activation, LOW[0:64, 0, :], LOW[0:64, 0, :], ACT.Tanh)
        t = act.do(A.activation, LOW[:, 1:3, :], LOW[:, 1:3, :], ACT.Sigmoid)
        pe.wait(t)
        R, K, Vv = region(A1, DT, S), region(A1 + 4096, DT, S), region(A1 + 8192, DT, S)
        AT, BB = region(A1 + 12288, DT, S), region(A1 + 16384, DT, S)
        BON = X
        f = [region(TMP + i * S, 1, S)[:, 0, :] for i in range(20)]
        PC = sml[:, 32:32 + DT * NCH].rearrange("p (c j) -> p c j", j=DT)
        ka1 = sml[:, 24:32]
        t = dve.do(V.tensor_scalar, ka1, p1("k_a", 0, 8), -1.0, 1.0, ALU.mult, ALU.add)
        act.wait(t)
        prev = [[], []]
        for j in range(DT):
            o = 10 * (j % 2)
            sg, ia, Lc, eP, eN, eM, kk0, sq, rn, t3 = f[o:o + 10]
            bw, ba, bs_ = (0, 1, 2) if j % 2 == 0 else (3, 4, 5)
            pw = prev[j % 2]
            pe.wait(*pw)
            w, first = w_tiles()
            mm(ps[:, bw, :], w[0:64, :], LOW[0:64, 0, :], True, True, first=first)
            m = mm_last(ps[:, ba, :], w[64:128, :], LOW[64:128, 0, :], True, True)
            t = act.do(A.activation, sg, ps[:, bw, :], ACT.Sigmoid, bias=p1("w0", j), w=[m, *pw])
            ti = act.do(A.activation, ia, ps[:, ba, :], ACT.Sigmoid, bias=p1("a0", j), w=m)
            dve.do(V.tensor_scalar, sg, sg, -DECAY_C, None, ALU.mult, w=t)
            tl = dve.do(V.tensor_tensor_scan, Lc, con[:, CONST["segs"]:CONST["segs"] + S], sg, 0.0, ALU.mult, ALU.add)
            td = pool.do(G.tensor_tensor, eM, Lc, sg, ALU.subtract, w=tl)
            act.do(A.activation, eP, Lc, ACT.Exp, w=tl)
            act.do(A.activation, eN, Lc, ACT.Exp, scale=-1.0)
            te = act.do(A.activation, eM, eM, ACT.Exp, w=td)
            tk = dve.do(V.tensor_scalar, kk0, K[:, j, :], p1("k_k", j), None, ALU.mult)
            tq = act.do(A.activation, sq, kk0, ACT.Square, w=tk)
            m = mm_last(ps[:, bs_, :], c_("blk"), sq, True, True, w=tq)
            tn = dve.do(V.tensor_scalar, rn, ps[:, bs_, :], 1e-24, None, ALU.max, w=m)
            tn = act.do(A.activation, rn, rn, ACT.Sqrt, w=tn)
            dve.do(V.reciprocal, rn, rn, w=tn)
            dve.do(V.tensor_tensor, kk0, kk0, rn, ALU.mult)
            dve.do(V.scalar_tensor_tensor, AT[:, j, :], kk0, -1.0, eM, ALU.mult, ALU.mult, w=te)
            dve.do(V.tensor_tensor, kk0, kk0, ia, ALU.mult, w=ti)
            dve.do(V.tensor_tensor, BB[:, j, :], kk0, eN, ALU.mult)
            dve.do(V.tensor_scalar, t3, ia, p1("k_a", j), ka1[:, j:j + 1], ALU.mult, ALU.add)
            dve.do(V.tensor_tensor, K[:, j, :], K[:, j, :], t3, ALU.mult)
            tb = dve.do(V.scalar_tensor_tensor, t3, R[:, j, :], p1("r_k", j), K[:, j, :], ALU.mult, ALU.mult)
            m = mm_last(ps[:, bs_, :], c_("blk"), t3, True, True, w=tb)
            dve.do(V.tensor_tensor, BON[:, j, 0:S], ps[:, bs_, :], Vv[:, j, :], ALU.mult, w=m)
            dve.do(V.tensor_tensor, K[:, j, :], K[:, j, :], eN, ALU.mult)
            t = dve.do(V.tensor_tensor, R[:, j, :], R[:, j, :], eP, ALU.mult)
            t2_ = dve.do(V.tensor_copy, PC[:, :, j], eP.rearrange("p (c s) -> p c s", s=CH)[:, :, CH - 1])
            prev[j % 2] = [t, t2_, m]
        dump("at", AT)
        dump("bb", BB)
        dump("kb", K)
        dump("rt", R)
        dump("bon", BON[:, :, 0:S])
        k.fence()

        HS = 512

        def chunk_buf(n, *shape):
            return region(TMP + n * HS, *shape)
        cAR = chunk_buf(0, DT, 2, CH)
        cB, cK, cV = (chunk_buf(2 + i, DT, CH) for i in range(3))
        XA, YA, XB, YB = (chunk_buf(5 + i, DT, CH) for i in range(4))
        PA, PB, QA, QB = (chunk_buf(9 + i, DT, CH) for i in range(4))
        OT, ARB, AAK, ARK = (chunk_buf(13 + i, DT, CH) for i in range(4))
        tB, tK, tV = (chunk_buf(17 + i, DT, CH) for i in range(3))
        RR, UU, ST = (chunk_buf(20 + i, DT, CH) for i in range(3))
        dve.do(V.memset, ST, 0.0)
        k.fence()

        def heads(bank, terms, w, width=CH, wide=1):
            pe.wait(*w)
            for j in range(DT):
                for u in range(2):
                    rows = slice(64 * u, 64 * u + 64)
                    col = j * width
                    o = ps[rows, bank + col // 512, col % 512:col % 512 + width]
                    for n, (lt, rh) in enumerate(terms):
                        lhs = lt[rows, j] if lt is not None else None
                        r = rh[rows, j] if len(rh.shape) > 2 else rh[rows]
                        if len(r.shape) == 3:
                            r = r.rearrange("p a c -> p (a c)")
                        if len(lhs.shape) == 3:
                            lhs = lhs.rearrange("p a c -> p (a c)")
                        args = (o, lhs, r, n == 0, n == len(terms) - 1)
                        if j == DT - 1 and u == 1 and n == len(terms) - 1:
                            return mm_last(*args)
                        mm(*args)

        def bank_v(b):
            return ps[:, b, :].rearrange("p (j c) -> p j c", c=CH)

        def masked(dst, bank2, part, mask, w):
            src = ps[:, bank2:bank2 + 2, :].rearrange("p b (j x c) -> p (b j) x c", x=2, c=CH)[:, :, part, :]
            return dve.do(V.tensor_tensor, dst, src, mask.unsqueeze(1).to_broadcast([P, DT, CH]), ALU.mult, w=w)

        def cm(name):
            return con[:, CONST[name]:CONST[name] + CH]

        def scan_chunk(c):
            cols = bass.ds(c * CH, CH)
            ta = pool.do(G.tensor_copy, cAR[:, :, 0, :], AT[:, :, cols])
            tr = act.do(A.copy, cAR[:, :, 1, :], R[:, :, cols])
            tb = dve.do(V.tensor_copy, cB, BB[:, :, cols])
            tk = act.do(A.copy, cK, K[:, :, cols])
            tv = pool.do(G.tensor_copy, cV, Vv[:, :, cols])
            cA = cAR[:, :, 0, :]
            cR = cAR[:, :, 1, :]
            m = heads(0, [(cB, cAR)], [ta, tr, tb], width=128)
            m2 = heads(4, [(cA, cB)], [])
            m1 = heads(2, [(cK, cAR)], [tk], width=128)
            eye = cm("eye64")
            m3 = heads(5, [(cB, eye)], [])
            heads(6, [(cK, eye)], [])
            m4 = heads(7, [(cV, eye)], [tv])
            yb = masked(YA, 0, 0, cm("m_diagT"), [m])
            xb = dve.do(V.tensor_tensor, XA, bank_v(4), cm("m_diag").unsqueeze(1).to_broadcast([P, DT, CH]),
                        ALU.mult, w=m2)
            eyeb = eye.unsqueeze(1).to_broadcast([P, DT, CH])
            g1 = pool.do(G.tensor_tensor, PA, XA, eyeb, ALU.add, w=xb)
            g2 = pool.do(G.tensor_tensor, QA, YA, eyeb, ALU.add, w=yb)
            masked(OT, 0, 0, cm("m_offT"), [])
            b0 = masked(ARB, 0, 1, cm("m_incT"), [])
            masked(AAK, 2, 0, cm("m_strT"), [m1])
            b2 = masked(ARK, 2, 1, cm("m_incT"), [])
            act.do(A.copy, tB, bank_v(5), w=m3)
            act.do(A.copy, tK, bank_v(6), w=m4)
            b5 = act.do(A.copy, tV, bank_v(7))
            q0 = heads(0, [(YA, XA)], [xb, yb, b0, b2])
            q1 = heads(1, [(XA, YA)], [])
            e0 = dve.do(V.tensor_copy, XB, bank_v(0), w=q0)
            e1 = act.do(A.copy, YB, bank_v(1), w=q1)
            q0 = heads(2, [(YB, XB)], [e0, e1])
            q1 = heads(3, [(XB, YB)], [])
            q2 = heads(4, [(YB, PA)], [g1])
            q3 = heads(5, [(XB, QA)], [g2, b5])
            e0 = act.do(A.copy, XA, bank_v(2), w=[q0, g1])
            e1 = act.do(A.copy, YA, bank_v(3), w=[q1, g2])
            e2 = dve.do(V.tensor_tensor, PB, bank_v(4), PA, ALU.add, w=q2)
            e3 = dve.do(V.tensor_tensor, QB, bank_v(5), QA, ALU.add, w=q3)
            q0 = heads(0, [(YA, XA)], [e0, e1])
            q1 = heads(1, [(XA, YA)], [])
            q2 = heads(6, [(YA, PB)], [e2])
            q3 = heads(7, [(XA, QB)], [e3])
            e0 = act.do(A.copy, XB, bank_v(0), w=q0)
            e1 = act.do(A.copy, YB, bank_v(1), w=q1)
            e2 = dve.do(V.tensor_tensor, PA, bank_v(6), PB, ALU.add, w=q2)
            e3 = dve.do(V.tensor_tensor, QA, bank_v(7), QB, ALU.add, w=q3)
            q2 = heads(4, [(YB, PA)], [e0, e1, e2])
            q3 = heads(5, [(XB, QA)], [e3])
            e2 = dve.do(V.tensor_tensor, PB, bank_v(4), PA, ALU.add, w=q2)
            e3 = dve.do(V.tensor_tensor, QB, bank_v(5), QA, ALU.add, w=q3)
            q0 = heads(2, [(OT, PB)], [e2])
            q1 = heads(3, [(PB, OT)], [])
            e0 = act.do(A.copy, XA, bank_v(2), w=q0)
            e1 = dve.do(V.tensor_copy, YA, bank_v(3), w=q1)
            q0 = heads(0, [(YA, XA)], [e0, e1])
            e0 = act.do(A.copy, XB, bank_v(0), w=q0)
            q0 = heads(1, [(XB, QB)], [e0, e3])
            e0 = dve.do(V.tensor_tensor, YB, bank_v(1), QB, ALU.add, w=q0)
            q0 = heads(4, [(XA, YB)], [e0])
            e4 = dve.do(V.tensor_tensor, QA, bank_v(4), YB, ALU.add, w=q0)
            q1 = heads(5, [(cA, ST), (AAK, tV)], [dve.done.now()])
            e5 = act.do(A.copy, RR, bank_v(5), w=q1)
            q2 = heads(6, [(QA, RR)], [e4, e5])
            e6 = act.do(A.copy, UU, bank_v(6), w=q2)
            q3 = heads(7, [(tB, UU), (tK, tV)], [e6])
            q4 = heads(2, [(ST, cR), (UU, ARB), (tV, ARK)], [])
            e7 = dve.do(V.tensor_tensor, ST, bank_v(7), ST, ALU.add, w=[q3, q4])
            pc = sml[:, bass.ds(c * DT + 32, DT)].unsqueeze(2).to_broadcast([P, DT, CH])
            dve.do(V.tensor_tensor, ST, ST, pc, ALU.mult)
            act.do(A.copy, R[:, :, cols], bank_v(2), w=q4)
        k.loop("chunks", NCH, scan_chunk)
        dump("y", R)

        Y = R
        prev = [[], []]
        for j in range(DT):
            o = 5 * (j % 2)
            sq, var, gg, c5, _ = f[o:o + 5]
            b0 = 3 * (j % 2)
            pe.wait(*prev[j % 2])
            m = mm_last(ps[:, b0, :], c_("blk_64"), Y[:, j, :], True, True)
            t = dve.do(V.tensor_tensor, Y[:, j, :], Y[:, j, :], ps[:, b0, :], ALU.subtract, w=m)
            t = act.do(A.activation, sq, Y[:, j, :], ACT.Square, w=[t, *prev[j % 2]])
            m = mm_last(ps[:, b0 + 1, :], c_("blk_64"), sq, True, True, w=t)
            w, first = w_tiles()
            w2_, first2 = w_tiles()
            mm(ps[:, b0 + 2, :], w, LOW[:, 1, :], True, False, first=first)
            mg = mm_last(ps[:, b0 + 2, :], w2_[0:32, :], LOW[0:32, 2, :], False, True)
            rsqrt(var, ps[:, b0 + 1, :], GN_EPS, w=m)
            dve.do(V.tensor_tensor, Y[:, j, :], Y[:, j, :], var, ALU.mult)
            dve.do(V.tensor_scalar, Y[:, j, :], Y[:, j, :], p1("gn_w", j), p1("gn_b", j), ALU.mult, ALU.add)
            dve.do(V.tensor_tensor, Y[:, j, :], Y[:, j, :], BON[:, j, 0:S], ALU.add)
            t = dve.do(V.tensor_tensor, Y[:, j, :], Y[:, j, :], ps[:, b0 + 2, :], ALU.mult, w=mg)
            prev[j % 2] = [t, act.done.now()]
        dump("yg", Y)
        k.fence()
        MA = region(A1 + 4096, DT, S)
        act.dma(ld_m, MA, m_spill.ap())
        act.dma(ld_x, X[:, :, 0:S], x_spill.ap())
        dve.wait(ld_m.now())
        MIX, Z = region(A1 + 12288, DT, S), region(A1 + 8192, DT, S)
        gated(Y, MIX, MA)
        k.fence()
        banks = Banks([0, 1, 2, 3])
        m_hi, m_lo = region_r(A1, DT, S), region_r(A1 + 12288, DT, S)
        lo_marks = halves(DT, lambda j: MIX[:, j, :], lambda j: m_hi[j], lambda j: m_lo[j])

        def ev_z(n, bs, mark):
            return [act.do(A.copy, Z[:, n, :], ps[:, bs[0], :], w=mark)]
        cut_up_to(64)
        linear3(DT, DT, lambda q, c0, cw: m_hi[q][:, c0:c0 + cw], lambda q, c0, cw: m_lo[q][:, c0:c0 + cw], SEG1,
                ev_z, banks, Cut(A1 + 29824), lambda q: lo_marks[q], False)
        pool.wait(ld_x.now())
        dve.wait(ld_x.now())
        add_normed(Z, lambda j: p1("post", j), 7, TMP)
        k.fence()
        dump("x1", X[:, :, 0:S])

        norm_to(H, SEG1, lambda j, si: p1("fpre", j), [7], TMP)
        k.fence()
        AC = region(A1, FT, S)
        ZF = region(A1 + FT * S, DT, S)
        TF = A1 + (FT + DT) * S
        ub = [region(TF + i * 520, 1, 520)[:, 0, :] for i in range(4)]
        cv = [region(TF + 2080 + i * S, 1, S)[:, 0, :] for i in range(4)]
        h_hi, h_lo = region_r(A1 + 19488, DT, S), region_r(6144, DT, S)
        for u in ub:
            dve.do(V.memset, u[:, 0:2], 0.0)
        spend_to_turn()
        halves(DT, lambda j: H[:, j, :], lambda j: h_hi[j], lambda j: h_lo[j])
        cut = Cut(A1 + 29824)
        cut.cut(Stream.pos // PIECE)
        k.fence()

        def ffn_pair(i):
            banks = Banks([0, 1, 2, 3])
            for s_ in range(4):
                banks.read[s_] = [k.before(f"u{s_}")]
            for w_ in range(2):
                cut.free[w_] = [*cut.free[w_], k.before(f"cut_used{w_}")]
            cut.ready[0] = [*cut.ready[0], k.before("cut_ready")]
            cut.ahead = Stream.pos // PIECE + 1
            for pr in range(2):
                q = i * 2 + pr

                def evac(h, bs, mark):
                    s_ = 2 * pr + h
                    u = ub[s_]
                    r = act.do(A.copy, u[:, 2:S + 2], ps[:, bs[0], :], w=[mark, k.before(f"conv{s_}")])
                    k.note(f"u{s_}", r)
                    at = q if h == 0 else q + FT

                    def col(base, step=0):
                        return par[:, bass.ds(at + (COLS1[base] + step), 1)]
                    dve.do(V.tensor_scalar, cv[s_], u[:, 2:S + 2], col("cw", 88), col("cb"), ALU.mult, ALU.add,
                           w=[r, k.before(f"mul{pr}")])
                    dve.do(V.scalar_tensor_tensor, cv[s_], u[:, 1:S + 1], col("cw", 44), cv[s_], ALU.mult, ALU.add)
                    c = dve.do(V.scalar_tensor_tensor, cv[s_], u[:, 0:S], col("cw", 0), cv[s_], ALU.mult, ALU.add)
                    k.note(f"conv{s_}", c)
                    if h == 0:
                        gelu[pr] = act.do(A.activation, cv[s_], cv[s_], ACT.Gelu_apprx_tanh, w=c)
                    else:
                        g = pool.do(G.tensor_tensor, AC[:, bass.ds(q, 1), :].rearrange("p a c -> p (a c)"), cv[s_],
                                    cv[s_ - 1], ALU.mult, w=[c, gelu[pr]])
                        k.note(f"mul{pr}", g)
                    return [r]
                gelu = {}
                linear3(2, DT, lambda q, c0, cw: h_hi[q][:, c0:c0 + cw], lambda q, c0, cw: h_lo[q][:, c0:c0 + cw],
                        SEG1, evac, banks, cut, lambda q: None, True)
            for w_ in range(2):
                k.note(f"cut_used{w_}", cut.free[w_][0])
            k.note("cut_ready", cut.ready[0][0])
        k.loop("ffn1", FT // 2, ffn_pair, fenced=False)
        cut.ahead = Stream.pos // PIECE + 1
        dump("acts", AC)
        a_hi, a_lo = region_r(A1 + 18560, FT, S), region_r(A1, FT, S)
        a_marks = halves(FT, lambda j: AC[:, j, :], lambda j: a_hi[j], lambda j: a_lo[j])

        def ev_zf(n, bs, mark):
            return [act.do(A.copy, ZF[:, n, :], ps[:, bs[0], :], w=mark)]
        cut_up_to(8 * FT + 80)
        linear3(DT, FT, lambda q, c0, cw: a_hi[q][:, c0:c0 + cw], lambda q, c0, cw: a_lo[q][:, c0:c0 + cw], SEG1,
                ev_zf, Banks([0, 1, 2, 3]), cut, lambda q: a_marks[q], False)
        k.fence()
        dump("zf", ZF)
        add_normed(ZF, lambda j: p1("fpost", j), 7, TF)
        k.fence()
        dump("x2", X[:, :, 0:S])

        PT_ = region(A1, 2, S)
        E = region(A1 + 1024, DT, S)
        act.dma(load_e, PT_, a["p"][bass.ds(layer, 1)].rearrange("a p t c -> p (a t) c"))
        for e in (act, dve):
            e.wait(load_e.now())
        p_hi, p_lo = region_r(A1 + 5120, 2, S), region_r(A1 + 6144, 2, S)
        x_hi, x_lo = region_r(A1 + 18560, DT, S), region_r(A1 + 22656, DT, S)
        pm = halves(2, lambda j: PT_[:, j, :], lambda j: p_hi[j], lambda j: p_lo[j])
        xm = halves(DT, lambda j: X[:, j, 0:S], lambda j: x_hi[j], lambda j: x_lo[j])
        banks = Banks([0, 1, 2, 3])
        gt2 = [region(TF + i * S, 1, S)[:, 0, :] for i in range(2)]
        used = [[], []]
        for n in range(DT):
            i = n % 2
            kept = {}

            def ev_e(_, bs, mark):
                kept["b"], kept["m"] = bs[0], mark
                return []
            linear3(1, 2, lambda q, c0, cw: p_hi[q][:, c0:c0 + cw], lambda q, c0, cw: p_lo[q][:, c0:c0 + cw], SEG1,
                    ev_e, banks, cut, lambda q: pm[q], False)

            def ev_g(_, bs, mark):
                g = act.do(A.activation, gt2[i], ps[:, bs[0], :], ACT.Sigmoid, w=[mark, *used[i]])
                r = dve.do(V.tensor_tensor, E[:, n, :], gt2[i], ps[:, kept["b"], :], ALU.mult, w=[g, kept["m"]])
                used[i] = [r]
                banks.read[kept["b"]] = [r]
                return [g]
            linear3(1, DT, lambda q, c0, cw: x_hi[q][:, c0:c0 + cw], lambda q, c0, cw: x_lo[q][:, c0:c0 + cw], SEG1,
                    ev_g, banks, cut, lambda q: xm[q], False)
        k.fence()
        add_normed(E, lambda j: p1("ple", j), 7, TF)
        spend_to_turn()
        k.fence()
        dump("x3", X[:, :, 0:S])

    def spend_to_turn():
        spend(-Stream.pos % TURN)

    def hybrid_loop(i):
        hybrid(i)
    start = Stream.pos
    k.loop("layers", L, hybrid_loop)
    Stream.pos = start
    k.fence()

    A2 = 12288
    H2 = region(6144, DT, T2)
    TB2 = A2 + 4 * 6144
    mods = sml[:, 100:196].rearrange("p (s c) -> p s c", c=2)
    gs = sml[:, 196:228]
    cond = sml[:, 228:244]
    act.dma(load_p, par[:, 0:NC2], a["par2"])
    for e in k.engines:
        e.wait(load_p.now())
    act.do(A.activation, cond, p2("cond", 0, 16), ACT.Silu)
    condv = cond.rearrange("p (q c) -> p q c", c=2)

    def modulation(layer):
        k.fence()
        row = [region(TB2 + 512 * i, 1, 512)[0:2, 0, :] for i in range(2)]
        used, back, bank_read = [[], []], [], [[], []]

        def turn_back(n, t):
            pe.wait(t)
            for q in range(4):
                m = mm_last(ps[:, 6, 8 * n + 2 * q:8 * n + 2 * q + 2], row[n % 2][:, q * P:(q + 1) * P],
                            c_("ident")[0:2, 0:2], True, True)
            used[n % 2] = [m]
            return m
        held = None
        for n in range(12):
            pe.wait(*bank_read[n % 2])
            for q in range(DT):
                w, first = w_tiles(4)
                args = (ps[0:2, n % 2, :], condv[:, q, :], w, q == 0, q == DT - 1)
                if q == DT - 1:
                    m = mm_last(*args)
                else:
                    mm(*args, first=first)
            t = act.do(A.copy, row[n % 2], ps[0:2, n % 2, :], w=[m, *used[n % 2]])
            bank_read[n % 2] = [t]
            if held:
                turn_back(*held)
            held = (n, t)
        m = turn_back(*held)
        b = p2("ada_b", 48 * layer, 48).unsqueeze(2).to_broadcast([P, 48, 2])
        dve.do(V.tensor_tensor, mods, ps[:, 6, 0:96].rearrange("p (s c) -> p s c", c=2), b, ALU.add, w=m)
        for which, norm in ((0, "norm1"), (1, "norm2")):
            g = p2(norm, 8 * layer, 8).unsqueeze(2).to_broadcast([P, 8, 2])
            sc = mods[:, 24 * which + 8:24 * which + 16, :]
            o = gs[:, 16 * which:16 * which + 16].rearrange("p (j c) -> p j c", c=2)
            dve.do(V.tensor_scalar, o, sc, 1.0, None, ALU.add)
            dve.do(V.tensor_tensor, o, o, g, ALU.mult)
        k.fence()

    def mod_norm(which, segs):
        norm_to(H2, segs, lambda j, si: gs[:, 16 * which + 2 * j + si:16 * which + 2 * j + si + 1],
                [6, 7], TB2, shift=lambda j, si: mods[:, 24 * which + j, si:si + 1])
        k.fence()

    h2_hi, h2_lo = region_r(A2 + 18432, DT, T2), region_r(6144, DT, T2)
    hh_ = lambda q, c0, cw: h2_hi[q][:, c0:c0 + cw]
    hl_ = lambda q, c0, cw: h2_lo[q][:, c0:c0 + cw]
    none = lambda q: None

    def cut_h2(wd):
        return halves(DT, lambda j: H2[:, j, 0:wd], lambda j: h2_hi[j][:, 0:wd], lambda j: h2_lo[j][:, 0:wd])

    def values_token_major(width, cols):
        k.fence()
        cut = Cut(TB2)
        n_rows = cols // (width * P)
        cut_up_to(n_rows * width * DT)
        for half in range(n_rows):
            for q in range(DT):
                hi, lo, first, whole = cut.tiles(width, (Stream.pos // PIECE + 1) * PIECE < cut_end[0])
                for tt in range(6):
                    toks = slice(tt * P, (tt + 1) * P)
                    o = ps[:, tt, 0:width * P]
                    mm(o, h2_hi[q][:, toks], hi, q == 0, False, first=first and tt == 0)
                    mm(o, h2_hi[q][:, toks], lo, False, False)
                    args = (o, h2_lo[q][:, toks], hi, False, q == DT - 1)
                    if tt == 5:
                        m = mm_last(*args)
                        cut.used(whole, m)
                    else:
                        mm(*args)
            for tt in range(6):
                t = act.do(A.copy, VTM[:, tt, half * 512:half * 512 + width * P], ps[:, tt, 0:width * P], w=m)
            pe.wait(t)
        k.fence()

    rope_ends = [[], []]

    def head_norm_rope(dst, n_tiles, gain, ones, rot, segs_of):
        raws = [region(TB2 + i * T2, 1, T2)[:, 0, :] for i in range(2)]
        sqs = [region(TB2 + (2 + i) * T2, 1, T2)[:, 0, :] for i in range(2)]
        rss = [region(TB2 + (4 + i) * T2, 1, T2)[:, 0, :] for i in range(2)]
        t1s = [region(TB2 + 6 * T2 + i * S, 1, S)[:, 0, :] for i in range(2)]
        wd = sum(c for _, c in segs_of)
        ends = rope_ends
        pending = []

        def finish(n, tq):
            i = n % 2
            raw, sq, rs, t1 = raws[i], sqs[i], rss[i], t1s[i]
            marks = []
            for si, (c0, cw) in enumerate(segs_of):
                m = mm_last(ps[:, 6 + si, 0:cw], ones, sq[:, c0:c0 + cw], True, True, w=[tq, dve.done.now()])
                marks.append(m)
            for si, (c0, cw) in enumerate(segs_of):
                dve.do(V.tensor_scalar, rs[:, c0:c0 + cw], ps[:, 6 + si, 0:cw], EPS, None, ALU.add, w=marks[si])
            t = act.do(A.activation, rs[:, 0:wd], rs[:, 0:wd], ACT.Sqrt, w=dve.done.now())
            dve.do(V.reciprocal, rs[:, 0:wd], rs[:, 0:wd], w=t)
            t = dve.do(V.scalar_tensor_tensor, raw[:, 0:wd], raw[:, 0:wd], gain, rs[:, 0:wd], ALU.mult, ALU.mult)
            if len(segs_of) > 1:
                pool.do(G.tensor_copy, dst[:, n, S:T2], raw[:, S:T2], w=t)
            m = mm_last(ps[:, 6, :], rot, raw[:, 0:S], True, True, w=t)
            c = pool.do(G.tensor_tensor, t1, raw[:, 0:S], tab[:, 0, :], ALU.mult, w=t)
            dve.do(V.tensor_tensor, sq[:, 0:S], ps[:, 6, :], tab[:, 1, :], ALU.mult, w=m)
            ends[i] = [dve.do(V.tensor_tensor, dst[:, n, 0:S], t1, sq[:, 0:S], ALU.add, w=c), c, m]

        def evac(n, bs, mark):
            i = n % 2
            r = []
            for si, (c0, cw) in enumerate(segs_of):
                r.append(act.do(A.copy, raws[i][:, c0:c0 + cw], ps[:, bs[si], 0:cw], w=[mark, *ends[i]]))
            t = act.do(A.activation, sqs[i][:, 0:wd], raws[i][:, 0:wd], ACT.Square)
            if pending:
                finish(*pending.pop())
            pending.append((n, t))
            if n == n_tiles - 1:
                finish(*pending.pop())
            return r
        return evac

    def add_gated(src_bank_linear, which, segs):
        def evac(n, bs, mark):
            r = []
            for si, (c0, cw) in enumerate(segs):
                r.append(dve.do(V.scalar_tensor_tensor, X[:, n, c0:c0 + cw], ps[:, bs[si], 0:cw],
                                mods[:, 24 * which + 16 + n, si:si + 1], X[:, n, c0:c0 + cw], ALU.mult, ALU.add,
                                w=mark))
            return r
        return evac

    def project_out(segs, banks):
        wd = sum(c for _, c in segs)
        o_hi, o_lo = region_r(A2, DT, T2), region_r(A2 + 18432, DT, T2)
        om = halves(DT, lambda j: O2[:, j, 0:wd], lambda j: o_hi[j][:, 0:wd], lambda j: o_lo[j][:, 0:wd])
        cut_up_to(64)
        linear3(DT, DT, lambda q, c0, cw: o_hi[q][:, c0:c0 + cw], lambda q, c0, cw: o_lo[q][:, c0:c0 + cw], segs,
                add_gated(None, 0, segs), banks, Cut(A2 + 6144), lambda q: om[q], False)

    def swiglu(segs):
        wd = sum(c for _, c in segs)
        hm = cut_h2(wd)
        cut = Cut(A2 + 27648)
        cut_up_to(24 * FT)
        AC = region(A2, FT, T2)
        g = [region(A2 + FT * T2 + i * T2, 1, T2)[:, 0, :] for i in range(2)]
        banks = Banks([0, 1, 2, 3] if len(segs) == 1 else [0, 1, 2, 3, 4, 5])
        used = [[], []]
        for n in range(FT):
            i = n % 2

            def evac(h, bs, mark):
                r = []
                for si, (c0, cw) in enumerate(segs):
                    if h == 0:
                        r.append(act.do(A.activation, g[i][:, c0:c0 + cw], ps[:, bs[si], 0:cw], ACT.Silu,
                                        w=[mark, *used[i]]))
                    else:
                        r.append(dve.do(V.tensor_tensor, AC[:, n, c0:c0 + cw], g[i][:, c0:c0 + cw],
                                        ps[:, bs[si], 0:cw], ALU.mult, w=[mark, act.done.now()]))
                        used[i] = [r[-1]]
                return r
            linear3(2, DT, hh_, hl_, segs, evac, banks, cut, (lambda q: hm[q]) if n == 0 else none, False)
        last = [pe.done.now(), dve.done.now()]
        a_lo = region_r(A2, FT, T2)
        part = [region_r(6144, DT, T2), region_r(A2 + FT * T2, FT - DT, T2)]
        a_hi = lambda j: part[0][j] if j < DT else part[1][j - DT]
        am = halves(FT, lambda j: AC[:, j, 0:wd], lambda j: a_hi(j)[:, 0:wd], lambda j: a_lo[j][:, 0:wd], w=last)
        linear3(DT, FT, lambda q, c0, cw: a_hi(q)[:, c0:c0 + cw], lambda q, c0, cw: a_lo[q][:, c0:c0 + cw], segs,
                add_gated(None, 1, segs), banks, cut, lambda q: am[q], False)
        k.fence()

    def attention_steps(steps, parts, scale, combine, values, out):
        n_parts = len(parts(steps[0]))
        E = [[region(TB2 + (2 * i + q) * T2, 1, T2)[:, 0, :] for q in range(2)] for i in range(2)]
        PTr = [region(TB2 + (4 + i) * T2, 6, P) for i in range(2)]
        stat = [[sml[:, 256 + 8 * i + 4 * q:260 + 8 * i + 4 * q] for q in range(2)] for i in range(2)]
        exp_read = [[], []]
        e_used, pt_used, o_used, t_read = [[], []], [[], []], [[], []], []
        ready, state, unit = {}, {}, 0

        def tail_transposes(s_):
            i = s_ % 2
            nb = state[s_] // P
            pe.wait(*ready[s_], *t_read)
            for b in range(nb):
                o = ps[:, 4 + b // 4, (b % 4) * P:(b % 4 + 1) * P]
                src = E[i][0][:, b * P:(b + 1) * P]
                if b == nb - 1:
                    m = pe.do(T.transpose, o, src, c_("ident"))
                else:
                    T.transpose(o, src, c_("ident"))
            e_used[i] = [m]
            n1 = min(nb, 4)
            r = [act.do(A.copy, PTr[i][:, 0:n1, :].rearrange("p a b -> p (a b)"), ps[:, 4, 0:n1 * P],
                        w=[m, *pt_used[i]])]
            if nb > 4:
                r.append(dve.do(V.tensor_copy, PTr[i][:, 4:nb, :].rearrange("p a b -> p (a b)"),
                                ps[:, 5, 0:(nb - 4) * P], w=[m, *pt_used[i]]))
            t_read[:] = r
            return r

        def tail_values(s_, copied):
            i = s_ % 2
            nb = state[s_] // P
            pe.wait(*copied, *o_used[i])
            for b in range(nb):
                args = (ps[:, 6 + i, 0:P], values(steps[s_], 6 - nb + b), PTr[i][:, b, :], b == 0, b == nb - 1)
                if b == nb - 1:
                    m = mm_last(*args)
                else:
                    mm(*args)
            pt_used[i] = [m]
            o_used[i] = [act.do(A.copy, out(steps[s_]), ps[:, 6 + i, 0:P], w=m)]

        for s_ in range(len(steps) + 1):
            if s_ < len(steps):
                i = s_ % 2
                todo = []
                for q, (qs, ks, s0) in enumerate(parts(steps[s_])):
                    bank = 2 * (unit % 2)
                    pe.wait(*exp_read[unit % 2])
                    for c0, cw, b in key_segments(s0, T2):
                        at = 0 if s0 else b
                        m = mm_last(ps[:, bank + at, 0:cw], qs, ks(c0, cw), True, True)
                    todo.append((q, bank, unit % 2, m))
                    unit += 1
                n = T2 - s0
                state[s_] = n
                scores = lambda bank: ps[:, bank:bank + 2, :].rearrange("p a b -> p (a b)")[:, 0:n]
                for q, bank, u, m in todo:
                    st_ = stat[i][q]
                    dve.do(V.tensor_reduce, st_[:, 0:1], scores(bank), AX_X, ALU.max, w=m)
                    t = dve.do(V.tensor_scalar, st_[:, 1:2], st_[:, 0:1], -scale, None, ALU.mult)
                    x = act.do(A.activation, E[i][q][:, 0:n], scores(bank), ACT.Exp, bias=st_[:, 1:2],
                               scale=scale, accum_out=st_[:, 2:3], w=[t, *e_used[i]])
                    exp_read[u] = [x]
            if s_ > 0:
                copied = tail_transposes(s_ - 1)
            if s_ < len(steps):
                for q in range(n_parts):
                    dve.do(V.reciprocal, stat[i][q][:, 2:3], stat[i][q][:, 2:3], w=x)
                ready[s_] = [combine(E[i], stat[i], n)]
            if s_ > 0:
                tail_values(s_ - 1, copied)

    def key_segments(s0, s1):
        out = []
        for c0, cw, b in ((0, S, 0), (S, CTX, 1)):
            lo, hi = max(s0, c0), min(s1, c0 + cw)
            if lo < hi:
                out.append((lo, hi - lo, b))
        return out

    Q2, K2, V2, O2 = (region(A2 + i * 6144, DT, T2) for i in range(4))
    VTM = region(A2 + 2 * 6144, 6, D)
    modulation(0)
    mod_norm(0, SEG2)
    act.dma(load_c, tab[:], a["tab64"])
    dve.wait(load_c.now())
    dump("h2", H2)
    banks = Banks([0, 1, 2, 3, 4, 5])
    hm = cut_h2(T2)
    cut = Cut(A2 + 2 * 6144)
    cut_up_to(128)
    linear3(DT, DT, hh_, hl_, SEG2, head_norm_rope(Q2, DT, p2("dq"), c_("blk_64"), c_("rot_ax64"), SEG2), banks,
            cut, lambda q: hm[q], False)
    linear3(DT, DT, hh_, hl_, SEG2, head_norm_rope(K2, DT, p2("dk"), c_("blk_64"), c_("rot_ax64"), SEG2), banks,
            cut, none, False)
    values_token_major(4, D)
    dump("q2", Q2)
    dump("k2", K2)
    lam = sml[:, 244:252]
    lv = p2("lam", 0, 4)
    dve.do(V.tensor_tensor, lam[:, 0:2], lv[:, 0:2], lv[:, 2:4], ALU.mult)
    m = mm_last(ps[:, 6, 0:2], c_("ones_128"), lam[:, 0:2], True, True, w=dve.done.now())
    t = act.do(A.activation, lam[:, 2:4], ps[:, 6, 0:2], ACT.Exp, scale=128.0, w=m)
    dve.do(V.tensor_tensor, lam[:, 4:5], lam[:, 2:3], lam[:, 3:4], ALU.subtract, w=t)
    dve.do(V.tensor_scalar, lam[:, 5:6], lam[:, 4:5], -1.0, -LAM_INIT, ALU.mult, ALU.add)
    dve.do(V.tensor_scalar, lam[:, 6:7], p2("subln"), 1.0 - LAM_INIT, None, ALU.mult)
    dump("lam", lam)
    k.fence()
    E0, E1 = region(TB2, 1, T2)[:, 0, :], region(TB2 + T2, 1, T2)[:, 0, :]

    def diff_parts(step):
        h, qt = step
        s0 = 0 if qt < 4 else S
        r = [slice(0, 64), slice(64, 128)]
        return [(Q2[r[u], h, qt * P:(qt + 1) * P], (lambda c0, cw, u=u: K2[r[u], h, c0:c0 + cw]), s0)
                for u in range(2)]

    def diff_combine(E, st_, n):
        dve.do(V.tensor_scalar, E[0][:, 0:n], E[0][:, 0:n], st_[0][:, 2:3], None, ALU.mult)
        dve.do(V.tensor_tensor, st_[1][:, 3:4], st_[1][:, 2:3], lam[:, 5:6], ALU.mult)
        return dve.do(V.scalar_tensor_tensor, E[0][:, 0:n], E[1][:, 0:n], st_[1][:, 3:4], E[0][:, 0:n],
                      ALU.mult, ALU.add)
    attention_steps([(h, qt) for h in range(DT) for qt in range(6)], diff_parts, 64 ** -0.5, diff_combine,
                    lambda step, b: VTM[:, b, step[0] * P:(step[0] + 1) * P],
                    lambda step: O2[:, step[0], step[1] * P:(step[1] + 1) * P])
    k.fence()
    dump("o2", O2)
    for h in range(DT):
        t = act.do(A.activation, E0, O2[:, h, :], ACT.Square, w=[dve.done.now(), pe.done.now()])
        for si, (c0, cw) in enumerate(SEG2):
            m = mm_last(ps[:, 6 + si, 0:cw], c_("ones_128"), E0[:, c0:c0 + cw], True, True, w=[t, dve.done.now()])
            rsqrt(E1[:, c0:c0 + cw], ps[:, 6 + si, 0:cw], EPS, w=m)
        dve.do(V.scalar_tensor_tensor, O2[:, h, :], O2[:, h, :], lam[:, 6:7], E1, ALU.mult, ALU.mult)
    k.fence()
    banks = Banks([0, 1, 2, 3, 4, 5])
    project_out(SEG2, banks)
    k.fence()
    dump("x4", X)
    mod_norm(1, SEG2)
    swiglu(SEG2)
    dump("x5", X)

    modulation(1)
    mod_norm(0, SEG2)
    act.dma(load_c, tab[:], a["tab128"], w=[dve.done.now()])
    dve.wait(load_c.now())
    banks = Banks([0, 1, 2, 3, 4, 5])
    hm = cut_h2(T2)
    cut = Cut(A2 + 2 * 6144)
    cut_up_to(80)
    linear3(DT, DT, hh_, hl_, SEG1, head_norm_rope(Q2, DT, p2("gq"), c_("ones_128"), c_("rot_ax128"), SEG1), banks,
            cut, lambda q: hm[q], False)
    linear3(2, DT, hh_, hl_, SEG2, head_norm_rope(K2, 2, p2("gk"), c_("ones_128"), c_("rot_ax128"), SEG2), banks,
            cut, none, False)
    values_token_major(2, 256)

    def gqa_parts(step):
        h, qt = step
        return [(Q2[:, h, qt * P:(qt + 1) * P], (lambda c0, cw: K2[:, h // 4, c0:c0 + cw]), 0)]

    def gqa_combine(E, st_, n):
        return dve.do(V.tensor_scalar, E[0], E[0], st_[0][:, 2:3], None, ALU.mult)
    attention_steps([(h, qt) for h in range(DT) for qt in range(4)], gqa_parts, 128 ** -0.5, gqa_combine,
                    lambda step, b: VTM[:, b, step[0] // 4 * P:(step[0] // 4 + 1) * P],
                    lambda step: O2[:, step[0], step[1] * P:(step[1] + 1) * P])
    k.fence()
    dump("o3", O2[:, :, 0:S])
    banks = Banks([0, 1, 2, 3])
    project_out(SEG1, banks)
    k.fence()
    mod_norm(1, SEG1)
    swiglu(SEG1)
    spend_to_turn()
    k.fence()
    act.dma(out_d, a["out"], X[:, :, 0:S])
    act.wait(out_d.now())
    act.do(A.copy, sml[:, 639:640], sml[:, 638:639])
    return k


def _tiles(w):
    kk, nn = w.shape
    return w.reshape(kk // P, P, nn // P, P).transpose(2, 0, 1, 3).reshape(-1, P, P)


def _rows(w, width):
    kk, nn = w.shape
    return (w.reshape(kk // P, P, nn // (width * P), width, P).transpose(2, 0, 3, 1, 4).reshape(-1, P, P))


def _inter(*ws):
    cols = [w.reshape(w.shape[0] // P, P, w.shape[1] // P, P).transpose(2, 0, 1, 3) for w in ws]
    return np.concatenate(cols, axis=1).reshape(-1, P, P)


def _feat(v):
    return v.reshape(-1, P).T


def _zeros(*shape):
    return np.zeros(shape, np.float32)


def _constants():
    con = np.zeros((P, NCONST), np.float32)

    def put(name, m):
        con[:, CONST[name]:CONST[name] + m.shape[1]] = m
    eye = np.eye(P, dtype=np.float32)
    blk = np.kron(np.eye(2), np.ones((64, 64)))
    put("ident", eye)
    put("ones_d", np.full((P, P), 1.0 / D))
    put("ones_128", np.full((P, P), 1.0 / P))
    put("blk", blk)
    put("blk_64", blk / 64)

    def rot(n, group, half):
        m = np.zeros((P, P))
        for i in range(P):
            if i % group < half:
                m[i + half, i] = -1.0
            else:
                m[i - half, i] = 1.0
        return m
    put("rot_nx", rot(P, 64, 32))
    put("rot_ax64", rot(P, 32, 16))
    put("rot_ax128", rot(P, 64, 32))
    s, t = np.meshgrid(np.arange(CH), np.arange(CH), indexing="ij")
    same = (s // 16) == (t // 16)
    two = lambda m: np.concatenate([m, m], axis=0).astype(np.float32)
    put("m_diagT", two((s < t) & same))
    put("m_offT", two((s < t) & ~same))
    put("m_diag", two((t < s) & same))
    put("m_incT", two(s <= t))
    put("m_strT", two(s < t))
    put("eye64", two(s == t))
    seg = np.ones((P, S))
    seg[:, ::CH] = 0
    put("segs", seg)
    q, kk = np.meshgrid(np.arange(P), np.arange(2 * P), indexing="ij")
    dist = q + P - kk
    put("band", np.where((dist >= 0) & (dist < P), 0.0, NEG))
    half = HD // 2
    inv = np.power(np.float32(10000.0), -np.arange(half, dtype=np.float32) / half)
    put("invf", np.tile(inv, 4)[:, None])
    return con


def _axial(dh):
    half = dh // 2
    inv = np.float32(10000.0) ** (-np.arange(0, half, 2, dtype=np.float32) / np.float32(half))
    pos = np.arange(S)
    r = (pos // 64).astype(np.float32)[:, None] * inv[None]
    c = (pos % 64).astype(np.float32)[:, None] * inv[None]
    ang = np.concatenate([r, r, c, c], axis=-1).astype(np.float32)
    n = P // dh
    return np.stack([np.tile(np.cos(ang).T, (n, 1)), np.tile(np.sin(ang).T, (n, 1))], axis=1).astype(np.float32)


def layout(i):
    f = {n: np.asarray(v) for n, v in i.items()}
    ws = []
    for l in range(L):
        w = f["w_in"][l]
        c = np.cumsum([0, 1024, 256, 256, 3072, 64, 64, 160, 1024, 1024])
        q, kk, v, rkv, wd, ad, gd, ga, gb = (w[:, c[n]:c[n + 1]] for n in range(9))
        ws += [_tiles(q), _tiles(kk), _rows(v, 2), _inter(ga, f["w_o_att"][l])]
        low = np.concatenate([wd, ad, gd, _zeros(D, 96)], axis=1)
        ws.append(_tiles(low))
        used = 64 + 16 + 16 + 128 + 24
        ws.append(_zeros(-used % TURN, P, P))
        ws.append(_tiles(rkv))
        used += -used % TURN + 192
        ws.append(_tiles(np.concatenate([f["rw_w2"][l], f["rw_a2"][l]], axis=0)))
        ws.append(_tiles(np.concatenate([f["rw_g2"][l], _zeros(96, D)], axis=0)))
        ws += [_inter(gb, f["w_o_rw"][l]), _tiles(f["w_out"][l])]
        used += 8 + 16 + 128 + 64
        ws.append(_zeros(-used % TURN, P, P))
        used += -used % TURN
        ws += [_inter(f["w_up"][l][:, :FFN], f["w_up"][l][:, FFN:]), _tiles(f["w_down"][l])]
        wp, wg = f["w_ple"][l], f["w_ple_gate"][l]
        ws.append(_inter(wp, wg))
        used += 24 * FT + 80
        ws.append(_zeros(-used % TURN, P, P))
    for l in range(2):
        ws.append(_rows(f["ada_w_2"][l], 4))
        if l == 0:
            w = f["diff_w_in_2"][0]
            ws += [_tiles(w[:, :2 * D]), _rows(w[:, 2 * D:], 4), _tiles(f["diff_w_out_2"][0])]
        else:
            w = f["gqa_w_in_2"][0]
            ws += [_tiles(w[:, :D + 256]), _rows(w[:, D + 256:], 2), _tiles(f["gqa_w_out_2"][0])]
        gu = f["ffn_w_gu_2"][l]
        ws += [_inter(gu[:, :FFN], gu[:, FFN:]), _tiles(f["ffn_w_down_2"][l])]
    n = sum(w.shape[0] for w in ws)
    ws.append(_zeros(-n % TURN, P, P))
    n += -n % TURN
    stream = np.concatenate(ws, axis=0).reshape(n // PIECE, PIECE, P, P).transpose(0, 2, 1, 3)
    par1 = np.zeros((L, P, NC1), np.float32)
    par2 = np.zeros((P, NC2), np.float32)

    def put1(l, name, m):
        par1[l, :, COLS1[name]:COLS1[name] + m.shape[1]] = m

    def put2(name, m):
        par2[:, COLS2[name]:COLS2[name] + m.shape[1]] = m
    for l in range(L):
        mu = f["rw_mu"][l]
        put1(l, "pre", _feat(f["norm_mix_pre"][l]))
        put1(l, "mu_rkv", _feat(mu[:3072]))
        put1(l, "mu_low", _feat(np.concatenate([mu[3072:], _zeros(96)])))
        for n_, s_ in (("w0", "rw_w0"), ("a0", "rw_a0"), ("k_k", "rw_k_k"), ("k_a", "rw_k_a"), ("gn_w", "rw_gn_w"),
                       ("gn_b", "rw_gn_b"), ("post", "norm_mix_post"), ("fpre", "norm_ffn_pre"),
                       ("cb", "conv_b"), ("fpost", "norm_ffn_post"), ("ple", "norm_ple")):
            put1(l, n_, _feat(f[s_][l]))
        put1(l, "r_k", _feat(f["rw_r_k"][l].reshape(-1)))
        put1(l, "cw", _feat(f["conv_w"][l].reshape(-1)))
        put1(l, "sinks", np.broadcast_to(f["att_sinks"][l].reshape(4, 2, 2).transpose(0, 2, 1).reshape(1, -1), (P, NQH)))
    put2("ada_b", np.concatenate([_feat(f["ada_b_2"][l]) for l in range(2)], axis=1))
    put2("norm1", np.concatenate([_feat(f["norm1_g_2"][l]) for l in range(2)], axis=1))
    put2("norm2", np.concatenate([_feat(f["norm2_g_2"][l]) for l in range(2)], axis=1))
    put2("dq", np.tile(f["diff_q_norm_2"][0], 2)[:, None])
    put2("dk", np.tile(f["diff_k_norm_2"][0], 2)[:, None])
    put2("gq", f["gqa_q_norm_2"][0][:, None])
    put2("gk", f["gqa_k_norm_2"][0][:, None])
    put2("subln", f["diff_subln_2"][0][:, None])
    lam = np.zeros((P, 4), np.float32)
    for n_, s_ in enumerate(("q1", "q2", "k1", "k2")):
        lam[:64, n_] = f[f"diff_lambda_{s_}_2"][0]
    put2("lam", lam)
    put2("cond", np.stack([_feat(f["c_2"][0]), _feat(f["c_ctx_2"])], axis=2).reshape(P, 16))

    def fm(x):
        return np.ascontiguousarray(x.T.reshape(-1, P, x.shape[0]).transpose(1, 0, 2))
    return {
        "w": np.ascontiguousarray(stream), "con": _constants(), "par1": par1, "par2": par2,
        "pos": np.ascontiguousarray(np.broadcast_to(f["positions"], (P, S))),
        "x": fm(f["x"][0]), "ctx": fm(f["ctx_2"][0]),
        "p": np.stack([fm(f["p"][l, 0]) for l in range(L)]),
        "tab64": _axial(64), "tab128": _axial(128),
    }


def _build(arrays, per, new_bass, probe=None):
    nc = new_bass()
    aps = {n: nc.dram_tensor("in_" + n, v.shape, mybir.dt.from_np(v.dtype), kind="ExternalInput").ap()
           for n, v in arrays.items()}
    aps["out"] = nc.dram_tensor("out_x", (P, DT, S), F32, kind="ExternalOutput").ap()
    for n, s in (probe or {}).items():
        aps["d_" + n] = nc.dram_tensor("dump_" + n, s, F32, kind="ExternalOutput").ap()
    k = program(nc, aps, per, probe)
    return nc, k


def kernel(**inputs):
    import concourse.bacc as bacc
    from concourse.bass_utils import run_bass_kernel_spmd

    def new_bass():
        return bacc.Bacc("TRN2", target_bir_lowering=False, num_devices=1)

    arrays = layout(inputs)
    _, counted = _build(arrays, {}, new_bass)
    nc, k = _build(arrays, counted.counted, new_bass)
    assert k.counted == counted.counted
    r = run_bass_kernel_spmd(nc, [{"in_" + n: v for n, v in arrays.items()}], core_ids=[0])
    out = r.results[0]["out_x"]
    return np.ascontiguousarray(out.transpose(1, 0, 2).reshape(D, S).T)[None]
```

```python
from contextlib import ExitStack

import numpy as np

import concourse.bass as bass
import concourse.mybir as mybir

F32 = mybir.dt.float32
F32R = mybir.dt.float32r
I32 = mybir.dt.int32
ALU = mybir.AluOpType
ACT = mybir.ActivationFunctionType
AX_X = mybir.AxisListType.X
ET = mybir.EngineType

P = 128
D = 1024
DT = D // P
S = 512
CTX = 256
T2 = S + CTX
L = 2
PLE = 256
FFN = 2816
FT = FFN // P
NQH, NKVH, HD = 16, 4, 64
CH = 64
NCH = S // CH
EPS = 1e-6
GN_EPS = 64e-5
NEG = -1e30
LAM_INIT = 0.8 - 0.6 * float(np.exp(-0.3 * 0))
DECAY_C = float(np.exp(-0.5))

PIECE = 8
SLOTS = 4

N_HYB = 64 + 16 + 16 + 128 + 24 + 192 + 8 + 16 + 128 + 64 + 16 * FT + 8 * FT + 80
TURN = PIECE * SLOTS
PAD_HYB = -N_HYB % TURN
N_DIFF = 384 + 64 + 64 + 64 + 64 + 16 * FT + 8 * FT
N_GQA = 384 + 64 + 16 + 16 + 64 + 16 * FT + 8 * FT
N_TILES = L * (N_HYB + PAD_HYB) + N_DIFF + N_GQA
N_TILES += -N_TILES % TURN

COLS1 = {}
_at = 0
for _n, _w in (("pre", 8), ("mu_rkv", 24), ("mu_low", 3), ("w0", 8), ("a0", 8), ("k_k", 8), ("k_a", 8),
               ("r_k", 8), ("gn_w", 8), ("gn_b", 8), ("post", 8), ("fpre", 8), ("cw", 132), ("cb", 44),
               ("fpost", 8), ("ple", 8), ("sinks", 16)):
    COLS1[_n] = _at
    _at += _w
NC1 = _at
COLS2 = {}
_at = 0
for _n, _w in (("ada_b", 96), ("norm1", 16), ("norm2", 16), ("dq", 1), ("dk", 1), ("gq", 1), ("gk", 1),
               ("subln", 1), ("lam", 4), ("cond", 16)):
    COLS2[_n] = _at
    _at += _w
NC2 = _at

CONST = {}
_at = 0
for _n, _w in (("ident", 128), ("ones_d", 128), ("ones_128", 128), ("blk", 128), ("blk_64", 128),
               ("rot_nx", 128), ("rot_ax64", 128), ("rot_ax128", 128), ("m_diagT", 64), ("m_offT", 64),
               ("m_diag", 64), ("m_incT", 64), ("m_strT", 64), ("eye64", 64), ("segs", 512),
               ("band", 256), ("invf", 1), ("sel", 30), ("sel_all", 30)):
    CONST[_n] = _at
    _at += _w
NCONST = _at


class Loop:
    def __init__(self, name, n, var):
        self.name, self.n, self.var, self.open = name, n, var, True


class Counter:

    def __init__(self, k, name):
        self.k, self.name = k, name
        self.sem = k.nc.alloc_semaphore(name)
        self.const = 0
        k.counters.append(self)

    def now(self):
        return (self, self.const, tuple((lp, self.k.per.get((lp.name, self.name), 0)) for lp in self.k.loops))


class Engine:

    def __init__(self, k, eng, name, chain=True):
        self.k, self.eng, self.name, self.chain = k, eng, name, chain
        self.done = Counter(k, f"{name}_done")
        self.tick = k.nc.alloc_semaphore(f"{name}_tick")
        self.seen = {}

    def wait(self, *marks):
        regs, consts = [], []
        for m in marks:
            if m is None:
                continue
            if isinstance(m, list):
                for x in m:
                    self.wait(x)
                continue
            c, const, coefs = m
            open_ = []
            for lp, per in coefs:
                if lp.open:
                    if per:
                        open_.append((lp, per))
                else:
                    const += per * (lp.n - 1)
            if const <= 0 and not open_:
                continue
            key = (c.name, tuple(lp.name for lp, _ in open_))
            if self.seen.get(key, -1) >= const:
                continue
            self.seen[key] = const
            (regs if open_ else consts).append((c, const, open_))
        for c, const, open_ in regs:
            v = const
            for lp, per in open_:
                v = lp.var * per + v
            self.eng.wait_ge(c.sem, v)
            self.eng.sem_inc(self.tick, 1)
        for c, const, _ in consts:
            self.eng.wait_ge(c.sem, const)

    def do(self, fn, *args, w=(), **kw):
        if self.chain:
            self.wait(self.done.now())
        self.wait(*w) if isinstance(w, (list, tuple)) and not (len(w) == 3 and isinstance(w[0], Counter)) else self.wait(w)
        self.done.const += 1
        fn(*args, **kw).then_inc(self.done.sem, 1)
        return self.done.now()

    def dma(self, counter, dst, src, w=()):
        self.wait(*w) if isinstance(w, (list, tuple)) and not (len(w) == 3 and isinstance(w[0], Counter)) else self.wait(w)
        self.eng.dma_start(dst, src).then_inc(counter.sem, 16)
        counter.const += 16
        return counter.now()


class Kit:
    def __init__(self, nc, per):
        self.nc, self.per = nc, per
        self.counted = {}
        self.counters, self.loops = [], []
        self.pe = Engine(self, nc.tensor, "pe", chain=False)
        self.act = Engine(self, nc.scalar, "act")
        self.dve = Engine(self, nc.vector, "dve")
        self.pool = Engine(self, nc.gpsimd, "pool")
        self.engines = (self.pe, self.act, self.dve, self.pool)

    def fence(self):
        marks = [e.done.now() for e in self.engines]
        for e in self.engines:
            e.wait(*[m for m in marks if m[0] is not e.done or e.chain])

    def note(self, name, mark):
        self.counted[("note", name)] = (mark[0].name, mark[1] - self.start[mark[0].name])

    def before(self, name):
        if ("note", name) not in self.per:
            return None
        c_name, local = self.per[("note", name)]
        c = next(c for c in self.counters if c.name == c_name)
        lp = self.loops[-1]
        const = self.start[c_name] + local - self.per[(lp.name, c_name)]
        assert const > 0
        now = c.now()
        return (c, const, now[2])

    def loop(self, name, n, body, fenced=True):
        start = {c.name: c.const for c in self.counters}
        self.start = start
        with self.nc.Fori(0, n, engines=(ET.PE, ET.Activation, ET.DVE, ET.Pool)) as i:
            lp = Loop(name, n, i)
            self.loops.append(lp)
            for e in self.engines:
                e.seen = {}
            if fenced:
                self.fence()
            body(i)
        self.loops.pop()
        lp.open = False
        for c in self.counters:
            one = c.const - start.get(c.name, 0)
            self.counted[(name, c.name)] = one
            c.const = start.get(c.name, 0) + one * n
        for e in self.engines:
            e.seen = {}
        self.fence()


def program(nc, a, per):
    k = Kit(nc, per)
    pe, act, dve, pool = k.pe, k.act, k.dve, k.pool
    V, A, G, T = nc.vector, nc.scalar, nc.gpsimd, nc.tensor

    ring = nc.alloc_sbuf_tensor("ring", [P, TURN, P], F32)
    big = nc.alloc_sbuf_tensor("big", [P, 44160], F32)
    con = nc.alloc_sbuf_tensor("con", [P, NCONST], F32)
    tab = nc.alloc_sbuf_tensor("tab", [P, 2, S], F32)
    par = nc.alloc_sbuf_tensor("par", [P, max(NC1, NC2)], F32)
    sml = nc.alloc_sbuf_tensor("sml", [P, 640], F32)
    ps = nc.alloc_psum_tensor("ps", [P, 8, 512], F32)
    x_spill = nc.dram_tensor("x_spill", [P, DT, S], F32)
    m_spill = nc.dram_tensor("m_spill", [P, DT, S], F32)
    h_spill = nc.dram_tensor("h_spill", [P, DT, S], F32)

    def region(at, *shape):
        n = int(np.prod(shape))
        assert at + n <= 44160, (at, shape)
        v = big[:, at:at + n]
        if len(shape) == 2:
            return v.rearrange("p (a b) -> p a b", b=shape[1])
        if len(shape) == 3:
            return v.rearrange("p (a b c) -> p a b c", b=shape[1], c=shape[2])
        return v

    rounded = {}

    def region_r(at, n, width):
        assert at + n * width <= 44160
        out = []
        for o in range(at, at + n * width, width):
            if (o, width) not in rounded:
                rounded[o, width] = nc.alloc_sbuf_tensor_at(f"rounded{o}_{width}", [P, width], F32R,
                                                            offset=nc.lookup_mloc(big).addr + 4 * o)
            out.append(rounded[o, width][:])
        return out

    X = region(0, DT, T2)

    def c_(name, w=None):
        return con[:, CONST[name]:CONST[name] + (w or 128)]

    def p1(name, j=0, w=1):
        return par[:, COLS1[name] + j:COLS1[name] + j + w]

    def p2(name, j=0, w=1):
        return par[:, COLS2[name] + j:COLS2[name] + j + w]

    full = [Counter(k, f"w_full{s}") for s in range(SLOTS)]
    freed = Counter(k, "w_freed")
    sp_tick = nc.alloc_semaphore("sp_tick")
    n_pieces = N_TILES // PIECE
    for s in range(SLOTS):
        nc.sync.dma_start(ring[:, s * PIECE:(s + 1) * PIECE, :], a["w"][s]).then_inc(full[s].sem, 16)
    with nc.sync.Fori(1, n_pieces // SLOTS) as turn:
        for s in range(SLOTS):
            nc.sync.wait_ge(freed.sem, turn * SLOTS + (s - SLOTS + 2))
            nc.sync.sem_inc(sp_tick, 1)
            nc.sync.dma_start(ring[:, s * PIECE:(s + 1) * PIECE, :],
                              a["w"][bass.ds(turn * SLOTS + s, 1)].rearrange("a p t c -> p (a t) c")
                              ).then_inc(full[s].sem, 16)

    class Stream:
        pos = 0

    def w_tiles(n=1):
        at = Stream.pos % TURN
        first = at % PIECE == 0
        assert at // PIECE == (at + n - 1) // PIECE
        if first:
            full[at // PIECE].const += 16
            pe.wait(full[at // PIECE].now())
        Stream.pos += n
        return ring[:, at:at + n, :].rearrange("p a b -> p (a b)"), first

    def mm(out, lhsT, rhs, start, stop, first=False, w=()):
        pe.wait(*w)
        i = T.matmul(out, lhsT, rhs, start=start, stop=stop, skip_group_check=True)
        if first:
            i.then_inc(freed.sem, 1)
            freed.const += 1

    def mm_last(out, lhsT, rhs, start, stop, w=()):
        return pe.do(T.matmul, out, lhsT, rhs, start=start, stop=stop, skip_group_check=True, w=w)

    class Banks:
        def __init__(self, ids):
            self.ids, self.i = ids, 0
            self.read = {b: [] for b in ids}

        def take(self):
            b = self.ids[self.i % len(self.ids)]
            self.i += 1
            return b

    def spend(pos_pad):
        for _ in range(pos_pad):
            w, first = w_tiles()
            if first:
                mm(ps[:, 7, 0:2], w, c_("ident")[:, 0:2], True, True, first=True)

    class Cut:

        def __init__(self, at):
            n = PIECE * P
            *self.hi, lo0, lo1 = region_r(at, 4, n)
            self.lo = [lo0, lo1]
            self.ready, self.free = [[], []], [[], []]
            self.ahead = None

        def cut(self, piece):
            slot, i = piece % SLOTS, piece % 2
            full[slot].const += 16
            raw = ring[:, slot * PIECE:(slot + 1) * PIECE, :].rearrange("p a b -> p (a b)")
            h = act.do(A.copy, self.hi[i], raw, w=[full[slot].now(), *self.free[i]])
            lo = dve.do(V.tensor_tensor, self.lo[i], raw, self.hi[i].bitcast(F32), ALU.subtract,
                        w=[full[slot].now(), h, *self.free[i]])
            self.ready[i] = [lo]
            self.ahead = piece + 1

        def tiles(self, n, more):
            at = Stream.pos % PIECE
            piece = Stream.pos // PIECE
            i = piece % 2
            first = at == 0
            if first:
                if self.ahead is None or self.ahead <= piece:
                    self.cut(piece)
                pe.wait(*self.ready[i])
                if more and self.ahead == piece + 1:
                    self.cut(piece + 1)
            assert at + n <= PIECE
            Stream.pos += n
            sl = slice(at * P, (at + n) * P)
            return self.hi[i][:, sl], self.lo[i][:, sl], first, (i if at + n == PIECE else None)

        def used(self, i, mark):
            if i is not None:
                self.free[i] = [mark]

    def linear3(n_out, kt, act_hi, act_lo, segs, evac, banks, cut, ready, more_after):
        for n in range(n_out):
            bs = [banks.take() for _ in segs]
            pe.wait(*[banks.read[b] for b in bs])
            for q in range(kt):
                more = more_after or (Stream.pos // PIECE + 1) * PIECE < cut_end[0]
                hi, lo, first, whole = cut.tiles(1, more)
                if n == 0:
                    pe.wait(ready(q))
                todo = [(si, w, x) for w, xs in ((hi, (act_hi, act_lo)), (lo, (act_hi,)))
                        for si in range(len(segs)) for x in xs]
                left = [sum(t[0] == si for t in todo) for si in range(len(segs))]
                for m_, (si, w, x) in enumerate(todo):
                    c0, cw = segs[si]
                    left[si] -= 1
                    args = (ps[:, bs[si], 0:cw], w, x(q, c0, cw), q == 0 and left[si] == 2,
                            q == kt - 1 and left[si] == 0)
                    if m_ == len(todo) - 1 and (q == kt - 1 or whole is not None):
                        mark = mm_last(*args)
                        cut.used(whole, mark)
                        after = Stream.pos // PIECE + 1
                        if whole is not None and (more_after or after * PIECE < cut_end[0]):
                            cut.cut(after)
                    else:
                        mm(*args, first=first and m_ == 0)
            r = evac(n, bs, mark)
            for b in bs:
                banks.read[b] = r

    cut_end = [0]

    def cut_up_to(tiles):
        cut_end[0] = Stream.pos + tiles

    def halves(n, raw, hi, lo, w=(), after=None):
        marks = []
        for j in range(n):
            h = act.do(A.copy, hi(j), raw(j), w=[*w, after[j] if after else None])
            marks.append(dve.do(V.tensor_tensor, lo(j), raw(j), hi(j).bitcast(F32), ALU.subtract, w=[h, *w]))
        return marks

    def sum_sq(src, n, segs, ones, bank_of, sq, ready=None):
        marks = [None, None]
        for j in range(n):
            t = act.do(A.activation, sq(j % 2), src(j), ACT.Square, w=[marks[j % 2], ready[j] if ready else None])
            for si, (c0, cw) in enumerate(segs):
                pe.wait(t)
                args = (ps[:, bank_of[si], 0:cw], ones, sq(j % 2)[:, c0:c0 + cw], j == 0, j == n - 1)
                if si == len(segs) - 1:
                    marks[j % 2] = mm_last(*args)
                else:
                    mm(*args)
        return marks[(n - 1) % 2]

    def rsqrt(dst, src, eps, w=()):
        t = dve.do(V.tensor_scalar, dst, src, eps, None, ALU.add, w=w)
        t = act.do(A.activation, dst, dst, ACT.Sqrt, w=t)
        return dve.do(V.reciprocal, dst, dst, w=t)

    SEG1 = [(0, S)]
    SEG2 = [(0, S), (S, CTX)]

    load_c = Counter(k, "load_const")
    load_x = Counter(k, "load_x")
    load_p = Counter(k, "load_par")
    load_e = Counter(k, "load_ple")
    st_x, ld_x = Counter(k, "store_x"), Counter(k, "reload_x")
    st_m, ld_m = Counter(k, "store_m"), Counter(k, "reload_m")
    st_h, ld_h = Counter(k, "store_h"), Counter(k, "reload_h")
    out_d = Counter(k, "store_out")
    act.dma(load_c, con[:], a["con"])
    act.dma(load_c, tab[:].bitcast(I32)[:, 0, :], a["pos"])
    act.dma(load_x, X[:, :, 0:S], a["x"])
    act.dma(load_x, X[:, :, S:T2], a["ctx"])
    for e in k.engines:
        e.wait(load_c.now(), load_x.now())

    TMP0 = 10240
    ang, nn, r_ = region(TMP0, 1, S)[:, 0, :], region(TMP0 + S, 1, S)[:, 0, :], region(TMP0 + 2 * S, 1, S)[:, 0, :]
    TWO_PI = 6.283185307179586
    C1 = 6.28125
    C2 = float(np.array(int(np.float32(TWO_PI - C1).view(np.int32)) >> 12 << 12, np.int32).view(np.float32))
    C3 = TWO_PI - C1 - C2
    MAGIC = 12582912.0
    dve.do(V.tensor_copy, ang, tab[:].bitcast(I32)[:, 0, :])
    dve.do(V.tensor_scalar, ang, ang, con[:, CONST["invf"]:CONST["invf"] + 1], None, ALU.mult)
    for which, shift in ((1, 0.0), (0, 0.25)):
        dve.do(V.tensor_scalar, nn, ang, 1.0 / TWO_PI, shift, ALU.mult, ALU.add)
        dve.do(V.tensor_scalar, nn, nn, MAGIC, MAGIC, ALU.add, ALU.subtract)
        dve.do(V.scalar_tensor_tensor, r_, nn, -C1, ang, ALU.mult, ALU.add)
        dve.do(V.scalar_tensor_tensor, r_, nn, -C2, r_, ALU.mult, ALU.add)
        dve.do(V.scalar_tensor_tensor, r_, nn, -C3, r_, ALU.mult, ALU.add)
        dve.do(V.tensor_scalar, r_, r_, shift * TWO_PI, None, ALU.add)
        t = dve.do(V.tensor_scalar, r_, r_, 3.14159, -3.14159, ALU.min, ALU.max)
        t = act.do(A.activation, tab[:, which, :], r_, ACT.Sin, w=t)
        dve.wait(t)
    COS, SIN = tab[:, 0, :], tab[:, 1, :]

    def norm_to(dst, segs, gain, bank_of, tmp_at, shift=None, ready=None, hi=None, lo=None):
        wd = sum(c for _, c in segs)
        sq = lambda i: region(tmp_at + i * wd, 1, wd)[:, 0, :]
        rs = region(tmp_at + 2 * wd, 1, wd)[:, 0, :]
        t = sum_sq(lambda j: X[:, j, 0:wd], DT, segs, c_("ones_d"), bank_of, sq, ready)
        for si, (c0, cw) in enumerate(segs):
            rsqrt(rs[:, c0:c0 + cw], ps[:, bank_of[si], 0:cw], EPS, w=t)
        marks, held = [], []

        def cut_lo(j, h):
            marks.append(dve.do(V.tensor_tensor, lo[j][:, 0:wd], dst[:, j, 0:wd], hi[j][:, 0:wd].bitcast(F32),
                                ALU.subtract, w=h))
        for j in range(DT):
            for si, (c0, cw) in enumerate(segs):
                t = dve.do(V.scalar_tensor_tensor, dst[:, j, c0:c0 + cw], X[:, j, c0:c0 + cw], gain(j, si),
                       rs[:, c0:c0 + cw], ALU.mult, ALU.mult)
                if shift is not None:
                    t = dve.do(V.tensor_scalar, dst[:, j, c0:c0 + cw], dst[:, j, c0:c0 + cw], shift(j, si), None,
                               ALU.add)
            last = t
            h = act.do(A.copy, hi[j][:, 0:wd], dst[:, j, 0:wd], w=t)
            held.append((j, h))
        for j, h in held:
            cut_lo(j, h)
        return last, marks

    def add_normed(Z, gain, bank, tmp_at, ready=None):
        sq = lambda i: region(tmp_at + i * S, 1, S)[:, 0, :]
        rs = sq(2)
        t = sum_sq(lambda j: Z[:, j, :], DT, SEG1, c_("ones_d"), [bank], sq, ready)
        rsqrt(rs, ps[:, bank, :], EPS, w=t)
        marks = []
        for j in range(DT):
            t = dve.do(V.scalar_tensor_tensor, Z[:, j, :], Z[:, j, :], gain(j), rs, ALU.mult, ALU.mult)
            marks.append(pool.do(G.tensor_tensor, X[:, j, 0:S], X[:, j, 0:S], Z[:, j, :], ALU.add, w=t))
        return marks

    A1 = 10240
    H = region(6144, DT, S)
    TMP = A1 + 20480

    def hybrid(layer):
        act.dma(load_p, par[:, 0:NC1], a["par1"][bass.ds(layer, 1)].rearrange("a p c -> p (a c)"))
        for e in k.engines:
            e.wait(load_p.now())
        act.dma(st_x, x_spill.ap(), X[:, :, 0:S])
        h_hi, h_lo = region_r(A1 + 16384, DT, S), region_r(TMP + 7680, DT, S)
        h_done, hm = norm_to(H, SEG1, lambda j, si: p1("pre", j), [7], TMP, hi=h_hi, lo=h_lo)
        act.dma(st_h, h_spill.ap(), H, w=[h_done])
        hh = lambda q, c0, cw: h_hi[q][:, c0:c0 + cw]
        hl = lambda q, c0, cw: h_lo[q][:, c0:c0 + cw]
        none = lambda q: None

        Q, O, KK, VT = (region(A1, DT, S), region(A1 + 4096, DT, S), region(A1 + 8192, 2, S),
                        region(A1 + 9216, 4, 256))
        M = region(A1 + 12288, DT, S)
        banks = Banks([0, 1, 2, 3])
        rot_read = {4: [], 5: []}
        raw = [region(TMP + i * S, 1, S)[:, 0, :] for i in range(2)]
        t1 = [region(TMP + (2 + i) * S, 1, S)[:, 0, :] for i in range(2)]
        t2 = [region(TMP + (4 + i) * S, 1, S)[:, 0, :] for i in range(2)]
        done = {"raw": [[], []], "t1": [[], []]}

        def rope_to(dst):
            def evac(n, bs, mark):
                i = n % 2
                r = act.do(A.copy, raw[i], ps[:, bs[0], :], w=[mark, *done["raw"][i]])
                m = mm_last(ps[:, 4 + i, :], c_("rot_nx"), raw[i], True, True, w=[r, *rot_read[4 + i]])
                c = pool.do(G.tensor_tensor, t1[i], raw[i], COS, ALU.mult, w=[r, *done["t1"][i]])
                s = dve.do(V.tensor_tensor, t2[i], ps[:, 4 + i, :], SIN, ALU.mult, w=m)
                rot_read[4 + i] = [s]
                f = dve.do(V.tensor_tensor, dst[:, n, :], t1[i], t2[i], ALU.add, w=c)
                done["t1"][i] = [f]
                done["raw"][i] = [c, m]
                return [r]
            return evac
        cut = Cut(A1 + 12288)
        cut_up_to(96)
        linear3(DT, DT, hh, hl, SEG1, rope_to(Q), banks, cut, lambda q: hm[q], False)
        linear3(2, DT, hh, hl, SEG1, rope_to(KK), banks, cut, none, False)
        pe.wait(*[banks.read[b] for b in banks.ids])
        for q in range(DT):
            hi, lo, first, whole = cut.tiles(2, (Stream.pos // PIECE + 1) * PIECE < cut_end[0])
            for tt in range(4):
                toks = slice(tt * P, (tt + 1) * P)
                o = ps[:, tt, 0:256]
                mm(o, h_hi[q][:, toks], hi, q == 0, False, first=first and tt == 0)
                mm(o, h_hi[q][:, toks], lo, False, False)
                m = mm_last(o, h_lo[q][:, toks], hi, False, q == DT - 1)
            cut.used(whole, m)
        t = act.do(A.copy, VT, ps[:, 0:4, 0:256], w=m)
        k.fence()

        sc_read, pt_read = [], []
        Pb = [region(TMP + 1024 * (1 + i), 4, 256) for i in range(2)]
        PT = [region(TMP + 1024 * (3 + i), 4, 256) for i in range(2)]
        pt_used = [[], []]
        o_read = {6: [], 7: []}
        pb_used = [[], []]

        def scores(n, g):
            k0 = max(n - 1, 0) * P
            kw = (n + 1) * P - k0
            pe.wait(*sc_read)
            for hh in range(4):
                h = 4 * g + hh
                qs = Q[64 * (h % 2):64 * (h % 2) + 64, h // 2, n * P:(n + 1) * P]
                ks = KD[h % 2][64 * (h % 2):64 * (h % 2) + 64, g, k0:k0 + kw]
                o = ps[:, hh % 2, (hh // 2) * 256 + 256 - kw:(hh // 2) * 256 + 256]
                if hh == 3:
                    return mm_last(o, qs, ks, True, True)
                mm(o, qs, ks, True, True)

        KDUP = region(TMP + 5120, 4, S)
        KD = (KDUP, KDUP)
        for g in range(4):
            src = KK[64 * (g % 2):64 * (g % 2) + 64, g // 2, :]
            for half in range(2):
                act.do(A.copy, KDUP[64 * half:64 * half + 64, g, :], src)
        k.fence()
        steps = [(n, g) for n in range(4) for g in range(4)]
        ready = {}
        Sb2 = [region(A1 + 12288 + 1024 * i, 4, 256) for i in range(2)]

        def span(n):
            kw = P if n == 0 else 256
            return kw, 256 - kw

        def softmax(it):
            n, g = steps[it]
            i = it % 2
            kw, lo = span(n)
            Sb = Sb2[i]
            mx, nm, sm, es = (sml[:, 16 * i + 4 * q:16 * i + 4 * q + 4] for q in range(4))
            band = con[:, CONST["band"] + lo:CONST["band"] + 256].unsqueeze(1).to_broadcast([P, 2, kw])
            for half in range(2):
                t = dve.do(V.tensor_tensor, Sb[:, 2 * half:2 * half + 2, lo:256],
                           ps[:, half, :].rearrange("p (h c) -> p h c", c=256)[:, :, lo:256], band, ALU.add,
                           w=[sc_mark[it], *s_used[i]])
            sc_read[:] = [t]
            dve.do(V.tensor_reduce, mx, Sb[:, :, lo:256], AX_X, ALU.max)
            sink = p1("sinks", 4 * g, 4)
            dve.do(V.scalar_tensor_tensor, mx, mx, HD ** -0.5, sink, ALU.mult, ALU.max)
            dve.do(V.tensor_scalar, nm, mx, -1.0, None, ALU.mult)
            t = dve.do(V.tensor_tensor, es, sink, mx, ALU.subtract)
            for hh in range(4):
                act.do(A.activation, Pb[i][:, hh, lo:256], Sb[:, hh, lo:256], ACT.Exp, bias=nm[:, hh:hh + 1],
                       scale=HD ** -0.5, accum_out=sm[:, hh:hh + 1], w=[t, *pb_used[i]])
            t = act.do(A.activation, es, es, ACT.Exp)
            s_used[i] = [t]
            return t

        def weigh(it, t):
            n, g = steps[it]
            i = it % 2
            kw, lo = span(n)
            sm, es = sml[:, 16 * i + 8:16 * i + 12], sml[:, 16 * i + 12:16 * i + 16]
            dve.do(V.tensor_tensor, sm, sm, es, ALU.add, w=t)
            t = dve.do(V.reciprocal, sm, sm)
            return pool.do(G.tensor_tensor, Pb[i][:, :, lo:256], Pb[i][:, :, lo:256],
                           sm.unsqueeze(2).to_broadcast([P, 4, kw]), ALU.mult, w=t)

        def turn(it):
            n, g = steps[it]
            i = it % 2
            kw, lo = span(n)
            pe.wait(ready[it], *pt_read)
            for hh in range(4):
                for b in range(kw // P):
                    o = ps[:, 2 + hh // 2, (hh % 2) * 256 + b * P:(hh % 2) * 256 + (b + 1) * P]
                    tp = Pb[i][:, hh, lo + b * P:lo + (b + 1) * P]
                    if hh == 3 and b == kw // P - 1:
                        m = pe.do(T.transpose, o, tp, c_("ident"))
                    else:
                        T.transpose(o, tp, c_("ident"))
            pb_used[i] = [m]
            r = []
            for half in range(2):
                e = act if half else dve
                f = A.copy if half else V.tensor_copy
                r.append(e.do(f, PT[i][:, 2 * half:2 * half + 2, 0:kw],
                              ps[:, 2 + half, :].rearrange("p (h c) -> p h c", c=256)[:, :, 0:kw],
                              w=[m, *pt_used[i]]))
            pt_read[:] = r

        def weighted_values(it):
            n, g = steps[it]
            i = it % 2
            kw, lo = span(n)
            bank = 6 + i
            pe.wait(*pt_read, *o_read[bank])
            for hh in range(4):
                half = hh % 2
                for b in range(kw // P):
                    vt = VT[:, (n if n == 0 else n - 1) + b, g * 64:(g + 1) * 64]
                    o = ps[64 * half:64 * half + 64, bank, (hh // 2) * P:(hh // 2 + 1) * P]
                    args = (o, vt, PT[i][:, 2 * (hh % 2) + hh // 2, b * P:(b + 1) * P], b == 0, b == kw // P - 1)
                    if hh == 3 and b == kw // P - 1:
                        m = mm_last(*args)
                    else:
                        mm(*args)
            pt_used[i] = [m]
            o_read[bank] = [act.do(A.copy, O[:, 2 * g:2 * g + 2, n * P:(n + 1) * P],
                                   ps[:, bank, 0:256].rearrange("p (a c) -> p a c", c=P), w=m)]

        sc_mark = {0: scores(*steps[0])}
        s_used = [[], []]
        for it in range(len(steps) + 1):
            if it < len(steps):
                t = softmax(it)
                if it + 1 < len(steps):
                    sc_mark[it + 1] = scores(*steps[it + 1])
            if it > 0:
                turn(it - 1)
            if it < len(steps):
                ready[it] = weigh(it, t)
            if it > 0:
                weighted_values(it - 1)
        k.fence()

        gt = [region(TMP + i * S, 1, S)[:, 0, :] for i in range(2)]

        def gated(h_hi, h_lo, s_hi, s_lo, ready, dst, extra=None):
            banks = Banks([0, 1, 2, 3])
            cut = Cut(TMP + 1024)
            cut_up_to(128)
            used = [[], []]
            for n in range(DT):
                i = n % 2

                def ev_gate(_, bs, mark):
                    return [act.do(A.activation, gt[i], ps[:, bs[0], :], ACT.Sigmoid, w=[mark, *used[i]])]

                def ev_y(_, bs, mark):
                    r = dve.do(V.tensor_tensor, dst[:, n, :] if extra is None else gt[i], ps[:, bs[0], :], gt[i],
                               ALU.mult, w=[mark, act.done.now()])
                    used[i] = [r]
                    if extra is not None:
                        used[i] = [dve.do(V.tensor_tensor, dst[:, n, :], gt[i], extra[:, n, :], ALU.add)]
                    return [r]
                linear3(1, DT, lambda q, c0, cw: h_hi[q][:, c0:c0 + cw], lambda q, c0, cw: h_lo[q][:, c0:c0 + cw],
                        SEG1, ev_gate, banks, cut, none, False)
                linear3(1, DT, lambda q, c0, cw: s_hi[q][:, c0:c0 + cw], lambda q, c0, cw: s_lo[q][:, c0:c0 + cw],
                        SEG1, ev_y, banks, cut, lambda q: ready[q], False)
        o_hi, o_lo = region_r(A1, DT, S), region_r(A1 + 8192, DT, S)
        om = halves(DT, lambda j: O[:, j, :], lambda j: o_hi[j], lambda j: o_lo[j])
        gated(h_hi, h_lo, o_hi, o_lo, om, M)
        k.fence()
        act.dma(st_m, m_spill.ap(), M)

        LOW = region(A1 + 32256, 3, S)
        RKV = region(A1, 3 * DT, S)
        zb = [region(TMP + i * 520, 1, 520)[:, 0, :] for i in range(2)]
        dd = [region(TMP + 1040 + i * S, 1, S)[:, 0, :] for i in range(2)]
        for i in range(2):
            t = dve.do(V.memset, zb[i][:, 0:1], 0.0)
        act.wait(t)

        def shifted(dst, mu):
            used = [[], []]

            def evac(n, bs, mark):
                i = n % 2
                r = act.do(A.copy, zb[i][:, 1:S + 1], ps[:, bs[0], :], w=[mark, *used[i]])
                d = pool.do(G.tensor_tensor, dd[i], zb[i][:, 0:S], zb[i][:, 1:S + 1], ALU.subtract, w=[r, *used[i]])
                u = dve.do(V.scalar_tensor_tensor, dst(n), dd[i], mu(n), zb[i][:, 1:S + 1],
                           ALU.mult, ALU.add, w=d)
                used[i] = [u]
                return [r]
            return evac
        banks = Banks([0, 1, 2, 3])
        cut = Cut(TMP + 2080)
        cut_up_to(24)
        linear3(3, DT, hh, hl, SEG1, shifted(lambda n: LOW[:, n, :], lambda n: p1("mu_low", n)), banks, cut,
                none, False)
        spend_to_turn()
        for e in k.engines:
            e.wait(st_m.now(), st_x.now())

        def rkv(i):
            b = Banks([0, 1, 2, 3])
            cut = Cut(TMP + 2080)
            cut_up_to(64)
            linear3(DT, DT, hh, hl, SEG1,
                   shifted(lambda n: RKV[:, bass.ds(i * DT + n, 1), :].rearrange("p a c -> p (a c)"),
                           lambda n: par[:, bass.ds(i * DT + (COLS1["mu_rkv"] + n), 1)]), b, cut, none, False)
        k.loop("rkv", 3, rkv)
        act.do(A.activation, LOW[0:64, 0, :], LOW[0:64, 0, :], ACT.Tanh)
        t = act.do(A.activation, LOW[:, 1:3, :], LOW[:, 1:3, :], ACT.Sigmoid)
        pe.wait(t)
        R, K, Vv = region(A1, DT, S), region(A1 + 4096, DT, S), region(A1 + 8192, DT, S)
        AT, BB = region(A1 + 12288, DT, S), region(A1 + 16384, DT, S)
        BON = X
        f = [region(TMP + i * S, 1, S)[:, 0, :] for i in range(22)]
        KN = region(6144, DT, S)
        PC = sml[:, 32:32 + DT * NCH].rearrange("p (c j) -> p c j", j=DT)
        ka1 = sml[:, 24:32]
        dve.wait(st_h.now())
        dve.do(V.tensor_scalar, ka1, p1("k_a", 0, 8), -1.0, 1.0, ALU.mult, ALU.add)
        spread = region(TMP + 18 * S, 2 * DT, 64)[0:2 * DT]

        def make_spread():
            return pool.do(G.tensor_copy, spread,
                           c_("ident")[0:2 * DT, 0:2 * DT].unsqueeze(2).to_broadcast([2 * DT, 2 * DT, 64]))

        def per_head(j, src, w):
            at = CONST["sel"] + 14 - 2 * j
            return mm_last(ps[0:2 * DT, 6, :], con[:, at:at + 2 * DT], src, j == 0, j == DT - 1, w=w)

        def spread_to(bank, j, rows, w):
            return mm_last(ps[:, bank, :], spread[:, 2 * j:2 * j + 2, :].rearrange("p a c -> p (a c)"), rows,
                           True, True, w=w)
        t_spread = make_spread()
        bank_read = [[], []]
        t_sq, t_sum, t_lc, t_ia, t_em = {}, {}, {}, {}, {}
        for j in range(DT):
            b0 = 2 * (j % 2)
            pe.wait(*bank_read[j % 2])
            w, first = w_tiles()
            mm(ps[:, b0, :], w[0:64, :], LOW[0:64, 0, :], True, True, first=first)
            m = mm_last(ps[:, b0 + 1, :], w[64:128, :], LOW[64:128, 0, :], True, True)
            t_sg = act.do(A.activation, AT[:, j, :], ps[:, b0, :], ACT.Sigmoid, bias=p1("w0", j), w=m)
            t_ia[j] = act.do(A.activation, BB[:, j, :], ps[:, b0 + 1, :], ACT.Sigmoid, bias=p1("a0", j))
            bank_read[j % 2] = [t_ia[j]]
            t = dve.do(V.tensor_scalar, KN[:, j, :], K[:, j, :], p1("k_k", j), None, ALU.mult)
            t_sq[j] = pool.do(G.tensor_tensor, f[j], KN[:, j, :], KN[:, j, :], ALU.mult, w=t)
            t_lc[j] = dve.do(V.tensor_tensor_scan, f[8 + j], con[:, CONST["segs"]:CONST["segs"] + S], AT[:, j, :],
                             0.0, ALU.mult, ALU.add, w=t_sg)
            t_em[j] = pool.do(G.tensor_tensor, AT[:, j, :], f[8 + j], AT[:, j, :], ALU.subtract, w=t_lc[j])
            if j > 0:
                t_sum[j - 1] = per_head(j - 1, f[j - 1], t_sq[j - 1])
        t_sum[DT - 1] = per_head(DT - 1, f[DT - 1], t_sq[DT - 1])
        rn = f[16][0:2 * DT, :]
        t = dve.do(V.tensor_scalar, rn, ps[0:2 * DT, 6, :], 1e-24, None, ALU.max, w=t_sum[DT - 1])
        t = act.do(A.activation, rn, rn, ACT.Sqrt, w=t)
        t_rn = dve.do(V.reciprocal, rn, rn, w=t)
        eP, eN = [f[17], f[20]], [f[21], region(TMP + 22 * S, 1, S)[:, 0, :]]
        e_used, kn_read, bon_read = [[], []], [[], []], [[], []]
        bonus = None
        for j in range(DT):
            i = j % 2
            act.do(A.activation, eP[i], f[8 + j], ACT.Exp, scale=-DECAY_C, w=[t_lc[j], *e_used[i]])
            act.do(A.activation, eN[i], f[8 + j], ACT.Exp, scale=DECAY_C)
            te = act.do(A.activation, AT[:, j, :], AT[:, j, :], ACT.Exp, scale=-DECAY_C, w=t_em[j])
            dve.do(V.tensor_scalar, f[j], BB[:, j, :], p1("k_a", j), ka1[:, j:j + 1], ALU.mult, ALU.add,
                   w=[t_sum[j], t_ia[j]])
            dve.do(V.tensor_tensor, K[:, j, :], K[:, j, :], f[j], ALU.mult)
            tb = dve.do(V.scalar_tensor_tensor, f[j], R[:, j, :], p1("r_k", j), K[:, j, :], ALU.mult, ALU.mult)
            mk = spread_to(i, j, rn, [t_rn, t_spread, *kn_read[i]])
            m = mm_last(ps[:, 4 + i, :], c_("blk"), f[j], True, True, w=[tb, *bon_read[i]])
            t = dve.do(V.tensor_tensor, KN[:, j, :], ps[:, i, :], KN[:, j, :], ALU.mult, w=mk)
            kn_read[i] = [t]
            ta = dve.do(V.scalar_tensor_tensor, AT[:, j, :], KN[:, j, :], -1.0, AT[:, j, :], ALU.mult, ALU.mult, w=te)
            pool.do(G.tensor_tensor, BB[:, j, :], KN[:, j, :], BB[:, j, :], ALU.mult, w=ta)
            pool.do(G.tensor_tensor, BB[:, j, :], BB[:, j, :], eN[i], ALU.mult, w=te)
            pool.do(G.tensor_tensor, K[:, j, :], K[:, j, :], eN[i], ALU.mult)
            tp = pool.do(G.tensor_copy, PC[:, :, j], eP[i].rearrange("p (c s) -> p c s", s=CH)[:, :, CH - 1])
            t = dve.do(V.tensor_tensor, R[:, j, :], R[:, j, :], eP[i], ALU.mult)
            e_used[i] = [t, tp]
            if bonus:
                jb, mb = bonus
                bon_read[jb % 2] = [dve.do(V.tensor_tensor, BON[:, jb, 0:S], ps[:, 4 + jb % 2, :], Vv[:, jb, :],
                                           ALU.mult, w=mb)]
            bonus = (j, m)
        jb, mb = bonus
        dve.do(V.tensor_tensor, BON[:, jb, 0:S], ps[:, 4 + jb % 2, :], Vv[:, jb, :], ALU.mult, w=mb)
        k.fence()

        GP = DT // 2
        NB = 14
        rooms = [6144 + n * GP * P for n in range(8)] + [TMP + n * GP * P for n in range(2 * NB - 8)]
        for x, at in enumerate(rooms):
            if x % 2:
                dve.do(V.memset, region(at, 1, GP * P), 0.0)
            else:
                pool.do(G.memset, region(at, 1, GP * P), 0.0)
        NAMES = ("AR", "cA", "cR", "B", "K", "V", "X", "Y", "Pw", "OT", "ARB", "AAK", "ARK", "ST")
        mats = [{n: region(rooms[NB * g + x], GP, P) for x, n in enumerate(NAMES)} for g in range(2)]
        k.fence()

        def block(m, u):
            return m[64 * u:64 * u + 64, :, 64 * u:64 * u + 64]

        def scan_group(g, turn, n_chunks):
            m_ = mats[g]
            AR, cA, cR, MB, MK, MV, MX, MY, PW, OT, ARB, AAK, ARK, ST = (m_[n] for n in NAMES)
            mine = slice(GP * g, GP * g + GP)
            read = {b: [] for b in range(4 * g, 4 * g + 4)}
            ident = c_("ident")
            ident_b = ident.unsqueeze(1).to_broadcast([P, GP, P])
            n_taken = [0]

            def product(*terms, w=()):
                b = 4 * g + n_taken[0] % 4
                n_taken[0] += 1
                pe.wait(*read[b], *w)
                for j in range(GP):
                    for n, (lt, rh) in enumerate(terms):
                        args = (ps[:, b, j * P:(j + 1) * P], lt[:, j, :], rh[:, j, :], n == 0, n == len(terms) - 1)
                        if j == GP - 1 and n == len(terms) - 1:
                            m = mm_last(*args)
                        else:
                            mm(*args)
                return b, m

            def transposed(src, w=()):
                b = 4 * g + n_taken[0] % 4
                n_taken[0] += 1
                pe.wait(*read[b], *w)
                for j in range(GP):
                    o = ps[:, b, j * P:(j + 1) * P]
                    if j == GP - 1:
                        m = pe.do(T.transpose, o, src[:, j, :], ident)
                    else:
                        T.transpose(o, src[:, j, :], ident)
                return b, m

            def out_of(b):
                return ps[:, b, :].rearrange("p (j c) -> p j c", c=P)

            def keep_act(dst, bm, w=()):
                b, m = bm
                read[b] = [act.do(A.copy, dst, out_of(b), w=[m, *w])]
                return read[b][0]

            def keep_dve(dst, bm, plus=None, w=()):
                b, m = bm
                if plus is None:
                    read[b] = [dve.do(V.tensor_copy, dst, out_of(b), w=[m, *w])]
                else:
                    read[b] = [dve.do(V.tensor_tensor, dst, out_of(b), plus, ALU.add, w=[m, *w])]
                return read[b][0]

            def masked(dst, bm, part, mask):
                b, m = bm
                for u in range(2):
                    rows = slice(64 * u, 64 * u + 64)
                    src = ps[rows, b, :].rearrange("p (j x c) -> p j x c", x=2, c=CH)[:, :, part, :]
                    mk = con[rows, CONST[mask]:CONST[mask] + CH].unsqueeze(1).to_broadcast([64, GP, CH])
                    t = dve.do(V.tensor_tensor, block(dst, u), src, mk, ALU.mult, w=m)
                read[b] = [t]
                return t

            end = None
            for sub in range(n_chunks):
                cols = bass.ds(turn * (n_chunks * CH) + sub * CH, CH)
                AR4 = AR.rearrange("p j (x c) -> p j x c", c=CH)
                t_ar = pool.do(G.tensor_copy, AR4[:, :, 0, :], AT[:, mine, cols], w=end)
                t_ar2 = act.do(A.copy, AR4[:, :, 1, :], R[:, mine, cols], w=end)

                def blocks_in(e, f, dst, src):
                    for u in range(2):
                        t = e.do(f, block(dst, u), src[64 * u:64 * u + 64, mine, cols], w=end)
                    return t
                t_b = blocks_in(dve, V.tensor_copy, MB, BB)
                t_k = blocks_in(act, A.copy, MK, K)
                t_a = blocks_in(pool, G.tensor_copy, cA, AT)
                t_r = blocks_in(act, A.copy, cR, R)
                t_v = blocks_in(pool, G.tensor_copy, MV, Vv)
                yield
                ba = product((MB, AR), w=[t_ar, t_ar2, t_b])
                ka = product((MK, AR), w=[t_k])
                t_y = masked(MY, ba, 0, "m_diagT")
                yield
                tb = transposed(MB)
                tx = transposed(MY, w=[t_y])
                masked(OT, ba, 0, "m_offT")
                t_arb = masked(ARB, ba, 1, "m_incT")
                t_x = keep_act(MX, tx)
                t_p = pool.do(G.tensor_tensor, PW, MX, ident_b, ALU.add, w=t_x)
                masked(AAK, ka, 0, "m_strT")
                t_ark = masked(ARK, ka, 1, "m_incT")
                yield
                x2 = product((MY, MX), w=[t_x])
                y2 = product((MX, MY))
                t_x = keep_act(MX, x2, w=[y2[1], t_p])
                t_y = keep_dve(MY, y2)
                t_tb = keep_act(MB, tb)
                yield
                y4 = product((MX, MY), w=[t_x, t_y])
                x4 = product((MY, MX))
                p2 = product((MY, PW), w=[t_p])
                t_y = keep_dve(MY, y4, w=[p2[1]])
                t_x = keep_act(MX, x4)
                t_p = keep_dve(PW, p2, PW, w=[t_p])
                tk = transposed(MK)
                t_tk = keep_act(MK, tk)
                yield
                y8 = product((MX, MY), w=[t_x, t_y])
                p3 = product((MY, PW), w=[t_p])
                t_y = keep_act(MY, y8, w=[p3[1]])
                t_p = keep_dve(PW, p3, PW)
                tv = transposed(MV, w=[t_v])
                t_tv = keep_act(MV, tv)
                yield
                p4 = product((MY, PW), w=[t_y, t_p])
                t_p = keep_dve(PW, p4, PW)
                rr = product((cA, ST), (AAK, MV), w=[t_a, t_ark, t_tv])
                t_rr = keep_act(AR, rr)
                yield
                h = product((OT, PW), w=[t_p])
                ht = product((PW, OT))
                q = transposed(PW)
                t_h = keep_act(MX, h)
                t_ht = keep_dve(MY, ht)
                t_q = keep_dve(PW, q)
                yield
                h2 = product((MY, MX), w=[t_h, t_ht])
                w1 = product((MX, PW), w=[t_q])
                t_h2 = keep_act(OT, h2)
                t_q = keep_dve(PW, w1, PW)
                yield
                w2 = product((OT, PW), w=[t_h2, t_q])
                t_q = keep_dve(PW, w2, PW)
                yield
                u_ = product((PW, AR), w=[t_q, t_rr])
                t_u = keep_act(MX, u_)
                yield
                st = product((MB, MX), (MK, MV), w=[t_u, t_tb, t_tk])
                yy = product((ST, cR), (MX, ARB), (MV, ARK), w=[t_r, t_arb, t_ark])
                t_st = keep_dve(ST, st, ST, w=[yy[1]])
                pc = sml[:, bass.ds(turn * (n_chunks * DT) + (sub * DT + 32 + GP * g), GP)]
                t_st = dve.do(V.tensor_tensor, ST, ST, pc.unsqueeze(2).to_broadcast([P, GP, P]), ALU.mult)
                for u in range(2):
                    rows = slice(64 * u, 64 * u + 64)
                    t = act.do(A.copy, R[rows, mine, cols],
                               ps[rows, yy[0], :].rearrange("p (j c) -> p j c", c=P)[:, :, 64 * u:64 * u + 64],
                               w=yy[1])
                read[yy[0]] = [t]
                pe.wait(t_st)
                end = yy[1]
                yield

        PER_TURN, LAG = 4, 5

        def scan_turn(i):
            first, second = (scan_group(g, i, PER_TURN) for g in range(2))
            for _ in range(LAG):
                next(first)
            for _ in second:
                next(first, None)
        k.loop("chunks", NCH // PER_TURN, scan_turn)

        act.dma(ld_h, H, h_spill.ap())
        Y = R
        t_spread = make_spread()
        bank_read = [[], []]
        t_sq = {}
        for j in range(DT):
            i = j % 2
            m = mm_last(ps[:, i, :], c_("blk_64"), Y[:, j, :], True, True, w=bank_read[i])
            t = dve.do(V.tensor_tensor, Y[:, j, :], Y[:, j, :], ps[:, i, :], ALU.subtract, w=m)
            bank_read[i] = [t]
            t_sq[j] = act.do(A.activation, f[j], Y[:, j, :], ACT.Square, w=t)
            if j > 0:
                per_head(j - 1, f[j - 1], t_sq[j - 1])
        m = per_head(DT - 1, f[DT - 1], t_sq[DT - 1])
        rv = f[16][0:2 * DT, :]
        t = dve.do(V.tensor_scalar, rv, ps[0:2 * DT, 6, :], 1.0 / HD, GN_EPS, ALU.mult, ALU.add, w=m)
        t = act.do(A.activation, rv, rv, ACT.Sqrt, w=t)
        t_rv = dve.do(V.reciprocal, rv, rv, w=t)
        var_read, gate_read = [[], []], [[], []]
        pend = None

        def gate(j, t, mg):
            gate_read[j % 2] = [dve.do(V.tensor_tensor, Y[:, j, :], Y[:, j, :], ps[:, 2 + j % 2, :], ALU.mult,
                                       w=[t, mg])]
        for j in range(DT):
            i = j % 2
            pe.wait(*gate_read[i])
            w, first = w_tiles()
            w2_, first2 = w_tiles()
            mm(ps[:, 2 + i, :], w, LOW[:, 1, :], True, False, first=first)
            mg = mm_last(ps[:, 2 + i, :], w2_[0:32, :], LOW[0:32, 2, :], False, True)
            m = spread_to(4 + i, j, rv, [t_rv, t_spread, *var_read[i]])
            t = dve.do(V.tensor_tensor, Y[:, j, :], Y[:, j, :], ps[:, 4 + i, :], ALU.mult, w=m)
            var_read[i] = [t]
            t = dve.do(V.tensor_scalar, Y[:, j, :], Y[:, j, :], p1("gn_w", j), p1("gn_b", j), ALU.mult, ALU.add)
            t = pool.do(G.tensor_tensor, Y[:, j, :], Y[:, j, :], BON[:, j, 0:S], ALU.add, w=t)
            if pend:
                gate(*pend)
            pend = (j, t, mg)
        gate(*pend)
        k.fence()
        MA = region(A1 + 4096, DT, S)
        act.dma(ld_m, MA, m_spill.ap())
        act.dma(ld_x, X[:, :, 0:S], x_spill.ap())
        for e in (act, dve):
            e.wait(ld_m.now(), ld_h.now())
        MIX, Z = region(A1 + 12288, DT, S), region(A1 + 8192, DT, S)
        h_hi, h_lo = region_r(A1 + 8192, DT, S), region_r(6144, DT, S)
        y_hi, y_lo = region_r(A1 + 16384, DT, S), region_r(A1, DT, S)
        hm = halves(DT, lambda j: H[:, j, :], lambda j: h_hi[j], lambda j: h_lo[j])
        pe.wait(hm[-1])
        ym = halves(DT, lambda j: Y[:, j, :], lambda j: y_hi[j], lambda j: y_lo[j])
        gated(h_hi, h_lo, y_hi, y_lo, ym, MIX, MA)
        k.fence()
        banks = Banks([0, 1, 2, 3])
        m_hi, m_lo = region_r(A1, DT, S), region_r(A1 + 12288, DT, S)
        lo_marks = halves(DT, lambda j: MIX[:, j, :], lambda j: m_hi[j], lambda j: m_lo[j])

        def ev_z(n, bs, mark):
            return [act.do(A.copy, Z[:, n, :], ps[:, bs[0], :], w=mark)]
        cut_up_to(64)
        linear3(DT, DT, lambda q, c0, cw: m_hi[q][:, c0:c0 + cw], lambda q, c0, cw: m_lo[q][:, c0:c0 + cw], SEG1,
                ev_z, banks, Cut(A1 + 29824), lambda q: lo_marks[q], False)
        pool.wait(ld_x.now())
        dve.wait(ld_x.now())
        x_marks = add_normed(Z, lambda j: p1("post", j), 7, TMP)

        h_hi, h_lo = region_r(A1 + 19488, DT, S), region_r(6144, DT, S)
        norm_to(H, SEG1, lambda j, si: p1("fpre", j), [6], A1 + 24000, ready=x_marks, hi=h_hi, lo=h_lo)
        AC = region(A1, FT, S)
        ZF = region(A1 + FT * S, DT, S)
        TF = A1 + (FT + DT) * S
        ub = [region(TF + i * 520, 1, 520)[:, 0, :] for i in range(4)]
        cv = [region(TF + 2080 + i * S, 1, S)[:, 0, :] for i in range(4)]
        for u in ub:
            dve.do(V.memset, u[:, 0:2], 0.0)
        spend_to_turn()
        cut = Cut(A1 + 29824)
        cut.cut(Stream.pos // PIECE)
        cut.cut(Stream.pos // PIECE + 1)
        k.fence()

        def ffn_pair(i):
            banks = Banks([0, 1, 2, 3])
            for s_ in range(4):
                banks.read[s_] = [k.before(f"u{s_}")]
            for w_ in range(2):
                cut.free[w_] = [*cut.free[w_], k.before(f"cut_used{w_}")]
                cut.ready[w_] = [*cut.ready[w_], k.before(f"cut_ready{w_}")]
            cut.ahead = Stream.pos // PIECE + 2
            for pr in range(2):
                q = i * 2 + pr

                def evac(h, bs, mark):
                    s_ = 2 * pr + h
                    u = ub[s_]
                    r = act.do(A.copy, u[:, 2:S + 2], ps[:, bs[0], :], w=[mark, k.before(f"conv{s_}")])
                    k.note(f"u{s_}", r)
                    at = q if h == 0 else q + FT

                    def col(base, step=0):
                        return par[:, bass.ds(at + (COLS1[base] + step), 1)]
                    dve.do(V.tensor_scalar, cv[s_], u[:, 2:S + 2], col("cw", 88), col("cb"), ALU.mult, ALU.add,
                           w=[r, k.before(f"mul{pr}")])
                    dve.do(V.scalar_tensor_tensor, cv[s_], u[:, 1:S + 1], col("cw", 44), cv[s_], ALU.mult, ALU.add)
                    c = dve.do(V.scalar_tensor_tensor, cv[s_], u[:, 0:S], col("cw", 0), cv[s_], ALU.mult, ALU.add)
                    k.note(f"conv{s_}", c)
                    if h == 0:
                        gelu[pr] = act.do(A.activation, cv[s_], cv[s_], ACT.Gelu_apprx_tanh, w=c)
                    else:
                        g = pool.do(G.tensor_tensor, AC[:, bass.ds(q, 1), :].rearrange("p a c -> p (a c)"), cv[s_],
                                    cv[s_ - 1], ALU.mult, w=[c, gelu[pr]])
                        k.note(f"mul{pr}", g)
                    return [r]
                gelu = {}
                linear3(2, DT, lambda q, c0, cw: h_hi[q][:, c0:c0 + cw], lambda q, c0, cw: h_lo[q][:, c0:c0 + cw],
                        SEG1, evac, banks, cut, lambda q: None, True)
            for w_ in range(2):
                k.note(f"cut_used{w_}", cut.free[w_][0])
                k.note(f"cut_ready{w_}", cut.ready[w_][0])
        k.loop("ffn1", FT // 2, ffn_pair, fenced=False)
        cut.ahead = Stream.pos // PIECE + 2
        a_hi, a_lo = region_r(A1 + 18560, FT, S), region_r(A1, FT, S)
        a_marks = halves(FT, lambda j: AC[:, j, :], lambda j: a_hi[j], lambda j: a_lo[j])

        def ev_zf(n, bs, mark):
            return [act.do(A.copy, ZF[:, n, :], ps[:, bs[0], :], w=mark)]
        cut_up_to(8 * FT + 80)
        linear3(DT, FT, lambda q, c0, cw: a_hi[q][:, c0:c0 + cw], lambda q, c0, cw: a_lo[q][:, c0:c0 + cw], SEG1,
                ev_zf, Banks([0, 1, 2, 3]), cut, lambda q: a_marks[q], False)

        PT_ = region(A1, 2, S)
        E = region(A1 + 1024, DT, S)
        act.dma(load_e, PT_, a["p"][bass.ds(layer, 1)].rearrange("a p t c -> p (a t) c"), w=[pe.done.now()])
        x_marks = add_normed(ZF, lambda j: p1("fpost", j), 7, TF)
        for e in (act, dve):
            e.wait(load_e.now())
        p_hi, p_lo = region_r(A1 + 5120, 2, S), region_r(A1 + 6144, 2, S)
        x_hi, x_lo = region_r(A1 + 18560, DT, S), region_r(A1 + 22656, DT, S)
        pm = halves(2, lambda j: PT_[:, j, :], lambda j: p_hi[j], lambda j: p_lo[j])
        xm = halves(DT, lambda j: X[:, j, 0:S], lambda j: x_hi[j], lambda j: x_lo[j],
                    after=x_marks)
        banks = Banks([0, 1, 2, 3])
        gt2 = [region(TF + i * S, 1, S)[:, 0, :] for i in range(2)]
        used = [[], []]
        e_marks = []
        for n in range(DT):
            i = n % 2
            kept = {}

            def ev_e(_, bs, mark):
                kept["b"], kept["m"] = bs[0], mark
                return []
            linear3(1, 2, lambda q, c0, cw: p_hi[q][:, c0:c0 + cw], lambda q, c0, cw: p_lo[q][:, c0:c0 + cw], SEG1,
                    ev_e, banks, cut, lambda q: pm[q], False)

            def ev_g(_, bs, mark):
                g = act.do(A.activation, gt2[i], ps[:, bs[0], :], ACT.Sigmoid, w=[mark, *used[i]])
                r = dve.do(V.tensor_tensor, E[:, n, :], gt2[i], ps[:, kept["b"], :], ALU.mult, w=[g, kept["m"]])
                used[i] = [r]
                e_marks.append(r)
                banks.read[kept["b"]] = [r]
                return [g]
            linear3(1, DT, lambda q, c0, cw: x_hi[q][:, c0:c0 + cw], lambda q, c0, cw: x_lo[q][:, c0:c0 + cw], SEG1,
                    ev_g, banks, cut, lambda q: xm[q], False)
        add_normed(E, lambda j: p1("ple", j), 7, TF + 2 * S, ready=e_marks)
        spend_to_turn()
        k.fence()

    def spend_to_turn():
        spend(-Stream.pos % TURN)

    def hybrid_loop(i):
        hybrid(i)
    start = Stream.pos
    k.loop("layers", L, hybrid_loop)
    Stream.pos = start
    k.fence()

    A2 = 12288
    H2 = region(6144, DT, T2)
    TB2 = A2 + 4 * 6144
    mods = sml[:, 100:196].rearrange("p (s c) -> p s c", c=2)
    gs = sml[:, 196:228]
    cond = sml[:, 228:244]
    act.dma(load_p, par[:, 0:NC2], a["par2"])
    for e in k.engines:
        e.wait(load_p.now())
    act.do(A.activation, cond, p2("cond", 0, 16), ACT.Silu)
    condv = cond.rearrange("p (q c) -> p q c", c=2)

    def modulation(layer):
        k.fence()
        row = [region(TB2 + 512 * i, 1, 512)[0:2, 0, :] for i in range(2)]
        used, back, bank_read = [[], []], [], [[], []]

        def turn_back(n, t):
            pe.wait(t)
            for q in range(4):
                m = mm_last(ps[:, 6, 8 * n + 2 * q:8 * n + 2 * q + 2], row[n % 2][:, q * P:(q + 1) * P],
                            c_("ident")[0:2, 0:2], True, True)
            used[n % 2] = [m]
            return m
        held = None
        for n in range(12):
            pe.wait(*bank_read[n % 2])
            for q in range(DT):
                w, first = w_tiles(4)
                args = (ps[0:2, n % 2, :], condv[:, q, :], w, q == 0, q == DT - 1)
                if q == DT - 1:
                    m = mm_last(*args)
                else:
                    mm(*args, first=first)
            t = act.do(A.copy, row[n % 2], ps[0:2, n % 2, :], w=[m, *used[n % 2]])
            bank_read[n % 2] = [t]
            if held:
                turn_back(*held)
            held = (n, t)
        m = turn_back(*held)
        b = p2("ada_b", 48 * layer, 48).unsqueeze(2).to_broadcast([P, 48, 2])
        dve.do(V.tensor_tensor, mods, ps[:, 6, 0:96].rearrange("p (s c) -> p s c", c=2), b, ALU.add, w=m)
        for which, norm in ((0, "norm1"), (1, "norm2")):
            g = p2(norm, 8 * layer, 8).unsqueeze(2).to_broadcast([P, 8, 2])
            sc = mods[:, 24 * which + 8:24 * which + 16, :]
            o = gs[:, 16 * which:16 * which + 16].rearrange("p (j c) -> p j c", c=2)
            dve.do(V.tensor_scalar, o, sc, 1.0, None, ALU.add)
            dve.do(V.tensor_tensor, o, o, g, ALU.mult)
        k.fence()

    def mod_norm(which, segs):
        return norm_to(H2, segs, lambda j, si: gs[:, 16 * which + 2 * j + si:16 * which + 2 * j + si + 1],
                       [6, 7], TB2, shift=lambda j, si: mods[:, 24 * which + j, si:si + 1],
                       hi=h2_hi, lo=h2_lo)[1]

    h2_hi, h2_lo = region_r(A2 + 18432, DT, T2), region_r(6144, DT, T2)
    hh_ = lambda q, c0, cw: h2_hi[q][:, c0:c0 + cw]
    hl_ = lambda q, c0, cw: h2_lo[q][:, c0:c0 + cw]
    none = lambda q: None

    def values_token_major(width, cols):
        k.fence()
        cut = Cut(TB2)
        n_rows = cols // (width * P)
        cut_up_to(n_rows * width * DT)
        for half in range(n_rows):
            for q in range(DT):
                hi, lo, first, whole = cut.tiles(width, (Stream.pos // PIECE + 1) * PIECE < cut_end[0])
                for tt in range(6):
                    toks = slice(tt * P, (tt + 1) * P)
                    o = ps[:, tt, 0:width * P]
                    mm(o, h2_hi[q][:, toks], hi, q == 0, False, first=first and tt == 0)
                    mm(o, h2_hi[q][:, toks], lo, False, False)
                    args = (o, h2_lo[q][:, toks], hi, False, q == DT - 1)
                    if tt == 5:
                        m = mm_last(*args)
                        cut.used(whole, m)
                    else:
                        mm(*args)
            for tt in range(6):
                t = act.do(A.copy, VTM[:, tt, half * 512:half * 512 + width * P], ps[:, tt, 0:width * P], w=m)
            pe.wait(t)
        k.fence()

    spread2 = region(TB2 + 6144, 2 * DT, 64)[0:2 * DT]

    def make_spread2():
        return pool.do(G.tensor_copy, spread2,
                       c_("ident")[0:2 * DT, 0:2 * DT].unsqueeze(2).to_broadcast([2 * DT, 2 * DT, 64]))

    class HeadNorm:

        def __init__(self, n_tiles, sel, segs, rows_at):
            self.n, self.sel, self.segs = n_tiles, sel, segs
            self.wd = sum(c for _, c in segs)
            self.rows = region(rows_at, 1, T2)[0:2 * DT, 0, :]
            self.sq = [region(TB2 + i * T2, 1, T2)[:, 0, :] for i in range(2)]
            self.sq_read, self.pending, self.before = [[], []], None, []

        def square(self, n, src, w):
            self.flush()
            t = act.do(A.activation, self.sq[n % 2][:, 0:self.wd], src, ACT.Square, w=[*w, *self.sq_read[n % 2]])
            self.pending = (n, t)

        def flush(self):
            if self.pending is None:
                return
            n, t = self.pending
            at = CONST[self.sel] + 14 - 2 * n
            for si, (c0, cw) in enumerate(self.segs):
                m = mm_last(ps[0:2 * DT, 6 + si, 0:cw], con[:, at:at + 2 * DT], self.sq[n % 2][:, c0:c0 + cw],
                            n == 0, n == self.n - 1, w=[t, *self.before])
            self.sq_read[n % 2] = [m]
            self.last, self.pending = m, None

        def root(self, width):
            self.flush()
            for si, (c0, cw) in enumerate(self.segs):
                t = dve.do(V.tensor_scalar, self.rows[:, c0:c0 + cw], ps[0:2 * DT, 6 + si, 0:cw], 1.0 / width, EPS,
                           ALU.mult, ALU.add, w=self.last)
            self.read = t
            t = act.do(A.activation, self.rows[:, 0:self.wd], self.rows[:, 0:self.wd], ACT.Sqrt, w=t)
            self.done = dve.do(V.reciprocal, self.rows[:, 0:self.wd], self.rows[:, 0:self.wd], w=t)

        def scale(self, n, tile, gain, pair, w):
            for si, (c0, cw) in enumerate(self.segs):
                m = mm_last(ps[:, pair[si], 0:cw], spread2[:, 2 * n:2 * n + 2, :].rearrange("p a c -> p (a c)"),
                            self.rows[:, c0:c0 + cw], True, True, w=[self.done, *w])
            for si, (c0, cw) in enumerate(self.segs):
                t = dve.do(V.scalar_tensor_tensor, tile[:, c0:c0 + cw], tile[:, c0:c0 + cw], gain,
                           ps[:, pair[si], 0:cw], ALU.mult, ALU.mult, w=m)
            return t

    def project_heads(parts, rot, sel, width, banks, cut, ready):
        t_spread = make_spread2()
        pe.wait(t_spread)
        t1s = [region(TB2 + 4 * T2 + i * S, 1, S)[:, 0, :] for i in range(2)]
        t2s = [region(TB2 + 4 * T2 + (2 + i) * S, 1, S)[:, 0, :] for i in range(2)]
        turn, used, pair_read = [0], [[], []], {4: []}
        todo = []

        def finish(hn, dst, gain, n, evac_marks):
            pair = pairs_[turn[0] % len(pairs_)]
            i = turn[0] % 2
            turn[0] += 1
            tile = dst[:, n, :]
            t = hn.scale(n, tile, gain, pair, [*pair_read[pair[0]], *evac_marks])
            m = mm_last(ps[:, pair[0], :], rot, tile[:, 0:S], True, True, w=t)
            c = pool.do(G.tensor_tensor, t1s[i], tile[:, 0:S], tab[:, 0, :], ALU.mult, w=[t, *used[i]])
            s_ = dve.do(V.tensor_tensor, t2s[i], ps[:, pair[0], :], tab[:, 1, :], ALU.mult, w=m)
            pair_read[pair[0]] = [s_]
            used[i] = [dve.do(V.tensor_tensor, tile[:, 0:S], t1s[i], t2s[i], ALU.add, w=c)]

        pairs_ = [(4, 5)]
        before = []
        for x, (dst, n_tiles, gain, segs) in enumerate(parts):
            hn = HeadNorm(n_tiles, sel, segs, TB2 + (2 + x) * T2)
            hn.before = before
            mine = []

            def evac(n, bs, mark):
                r = [act.do(A.copy, dst[:, n, c0:c0 + cw], ps[:, bs[si], 0:cw], w=mark)
                     for si, (c0, cw) in enumerate(segs)]
                hn.square(n, dst[:, n, 0:hn.wd], [])
                mine.append((hn, dst, gain, n, r))
                for _ in range(-(-len(todo) // (n_tiles - n))):
                    finish(*todo.pop(0))
                return r
            linear3(n_tiles, DT, hh_, hl_, segs, evac, banks, cut, ready if x == 0 else none, False)
            hn.root(width)
            before = [hn.read]
            todo = mine
        for b in (0, 2):
            pair_read[b] = [*banks.read[b], *banks.read[b + 1]]
        pairs_ = [(4, 5), (0, 1), (2, 3)]
        for t in todo:
            finish(*t)

    def add_gated(which, segs):
        def evac(n, bs, mark):
            r = []
            for si, (c0, cw) in enumerate(segs):
                r.append(dve.do(V.scalar_tensor_tensor, X[:, n, c0:c0 + cw], ps[:, bs[si], 0:cw],
                                mods[:, 24 * which + 16 + n, si:si + 1], X[:, n, c0:c0 + cw], ALU.mult, ALU.add,
                                w=mark))
            return r
        return evac

    def project_out(segs, banks):
        wd = sum(c for _, c in segs)
        o_hi, o_lo = region_r(A2, DT, T2), region_r(A2 + 18432, DT, T2)
        om = halves(DT, lambda j: O2[:, j, 0:wd], lambda j: o_hi[j][:, 0:wd], lambda j: o_lo[j][:, 0:wd])
        cut_up_to(64)
        linear3(DT, DT, lambda q, c0, cw: o_hi[q][:, c0:c0 + cw], lambda q, c0, cw: o_lo[q][:, c0:c0 + cw], segs,
                add_gated(0, segs), banks, Cut(A2 + 6144), lambda q: om[q], False)

    def swiglu(segs, hm):
        wd = sum(c for _, c in segs)
        cut = Cut(A2 + 27648)
        cut_up_to(24 * FT)
        AC = region(A2, FT, T2)
        g = [region(A2 + FT * T2 + i * T2, 1, T2)[:, 0, :] for i in range(2)]
        banks = Banks([0, 1, 2, 3] if len(segs) == 1 else [0, 1, 2, 3, 4, 5])
        used = [[], []]
        for n in range(FT):
            i = n % 2

            def evac(h, bs, mark):
                r = []
                for si, (c0, cw) in enumerate(segs):
                    if h == 0:
                        r.append(act.do(A.activation, g[i][:, c0:c0 + cw], ps[:, bs[si], 0:cw], ACT.Silu,
                                        w=[mark, *used[i]]))
                    else:
                        r.append(dve.do(V.tensor_tensor, AC[:, n, c0:c0 + cw], g[i][:, c0:c0 + cw],
                                        ps[:, bs[si], 0:cw], ALU.mult, w=[mark, act.done.now()]))
                        used[i] = [r[-1]]
                return r
            linear3(2, DT, hh_, hl_, segs, evac, banks, cut, (lambda q: hm[q]) if n == 0 else none, False)
        last = [pe.done.now(), dve.done.now()]
        a_lo = region_r(A2, FT, T2)
        part = [region_r(6144, DT, T2), region_r(A2 + FT * T2, FT - DT, T2)]
        a_hi = lambda j: part[0][j] if j < DT else part[1][j - DT]
        am = halves(FT, lambda j: AC[:, j, 0:wd], lambda j: a_hi(j)[:, 0:wd], lambda j: a_lo[j][:, 0:wd], w=last)
        linear3(DT, FT, lambda q, c0, cw: a_hi(q)[:, c0:c0 + cw], lambda q, c0, cw: a_lo[q][:, c0:c0 + cw], segs,
                add_gated(1, segs), banks, cut, lambda q: am[q], False)
        k.fence()

    def attention_steps(steps, parts, scale, combine, values, out):
        n_parts = len(parts(steps[0]))
        E = [[region(TB2 + (2 * i + q) * T2, 1, T2)[:, 0, :] for q in range(2)] for i in range(2)]
        PTr = [region(TB2 + (4 + i) * T2, 6, P) for i in range(2)]
        stat = [[sml[:, 256 + 8 * i + 4 * q:260 + 8 * i + 4 * q] for q in range(2)] for i in range(2)]
        exp_read = [[], []]
        e_used, pt_used, o_used, t_read = [[], []], [[], []], [[], []], []
        ready, state, unit = {}, {}, 0

        def tail_transposes(s_):
            i = s_ % 2
            nb = state[s_] // P
            pe.wait(*ready[s_], *t_read)
            for b in range(nb):
                o = ps[:, 4 + b // 4, (b % 4) * P:(b % 4 + 1) * P]
                src = E[i][0][:, b * P:(b + 1) * P]
                if b == nb - 1:
                    m = pe.do(T.transpose, o, src, c_("ident"))
                else:
                    T.transpose(o, src, c_("ident"))
            e_used[i] = [m]
            n1 = min(nb, 4)
            r = [act.do(A.copy, PTr[i][:, 0:n1, :].rearrange("p a b -> p (a b)"), ps[:, 4, 0:n1 * P],
                        w=[m, *pt_used[i]])]
            if nb > 4:
                r.append(dve.do(V.tensor_copy, PTr[i][:, 4:nb, :].rearrange("p a b -> p (a b)"),
                                ps[:, 5, 0:(nb - 4) * P], w=[m, *pt_used[i]]))
            t_read[:] = r
            return r

        def tail_values(s_, copied):
            i = s_ % 2
            nb = state[s_] // P
            pe.wait(*copied, *o_used[i])
            for b in range(nb):
                args = (ps[:, 6 + i, 0:P], values(steps[s_], 6 - nb + b), PTr[i][:, b, :], b == 0, b == nb - 1)
                if b == nb - 1:
                    m = mm_last(*args)
                else:
                    mm(*args)
            pt_used[i] = [m]
            o_used[i] = [act.do(A.copy, out(steps[s_]), ps[:, 6 + i, 0:P], w=m)]

        for s_ in range(len(steps) + 1):
            if s_ < len(steps):
                i = s_ % 2
                todo = []
                for q, (qs, ks, s0) in enumerate(parts(steps[s_])):
                    bank = 2 * (unit % 2)
                    pe.wait(*exp_read[unit % 2])
                    for c0, cw, b in key_segments(s0, T2):
                        at = 0 if s0 else b
                        m = mm_last(ps[:, bank + at, 0:cw], qs, ks(c0, cw), True, True)
                    todo.append((q, bank, unit % 2, m))
                    unit += 1
                n = T2 - s0
                state[s_] = n
                scores = lambda bank: ps[:, bank:bank + 2, :].rearrange("p a b -> p (a b)")[:, 0:n]
                for q, bank, u, m in todo:
                    st_ = stat[i][q]
                    dve.do(V.tensor_reduce, st_[:, 0:1], scores(bank), AX_X, ALU.max, w=m)
                    t = dve.do(V.tensor_scalar, st_[:, 1:2], st_[:, 0:1], -scale, None, ALU.mult)
                    x = act.do(A.activation, E[i][q][:, 0:n], scores(bank), ACT.Exp, bias=st_[:, 1:2],
                               scale=scale, accum_out=st_[:, 2:3], w=[t, *e_used[i]])
                    exp_read[u] = [x]
            if s_ > 0:
                copied = tail_transposes(s_ - 1)
            if s_ < len(steps):
                for q in range(n_parts):
                    dve.do(V.reciprocal, stat[i][q][:, 2:3], stat[i][q][:, 2:3], w=x)
                ready[s_] = [combine(E[i], stat[i], n)]
            if s_ > 0:
                tail_values(s_ - 1, copied)

    def key_segments(s0, s1):
        out = []
        for c0, cw, b in ((0, S, 0), (S, CTX, 1)):
            lo, hi = max(s0, c0), min(s1, c0 + cw)
            if lo < hi:
                out.append((lo, hi - lo, b))
        return out

    Q2, K2, V2, O2 = (region(A2 + i * 6144, DT, T2) for i in range(4))
    VTM = region(A2 + 2 * 6144, 6, D)
    modulation(0)
    hm = mod_norm(0, SEG2)
    act.dma(load_c, tab[:], a["tab64"])
    dve.wait(load_c.now())
    banks = Banks([0, 1, 2, 3])
    cut = Cut(A2 + 2 * 6144)
    cut_up_to(128)
    project_heads([(Q2, DT, p2("dq"), SEG2), (K2, DT, p2("dk"), SEG2)], c_("rot_ax64"), "sel", 64, banks, cut,
                  lambda q: hm[q])
    values_token_major(4, D)
    lam = sml[:, 244:252]
    lv = p2("lam", 0, 4)
    dve.do(V.tensor_tensor, lam[:, 0:2], lv[:, 0:2], lv[:, 2:4], ALU.mult)
    m = mm_last(ps[:, 6, 0:2], c_("ones_128"), lam[:, 0:2], True, True, w=dve.done.now())
    t = act.do(A.activation, lam[:, 2:4], ps[:, 6, 0:2], ACT.Exp, scale=128.0, w=m)
    dve.do(V.tensor_tensor, lam[:, 4:5], lam[:, 2:3], lam[:, 3:4], ALU.subtract, w=t)
    dve.do(V.tensor_scalar, lam[:, 5:6], lam[:, 4:5], -1.0, -LAM_INIT, ALU.mult, ALU.add)
    dve.do(V.tensor_scalar, lam[:, 6:7], p2("subln"), 1.0 - LAM_INIT, None, ALU.mult)
    k.fence()

    def diff_parts(step):
        h, qt = step
        s0 = 0 if qt < 4 else S
        r = [slice(0, 64), slice(64, 128)]
        return [(Q2[r[u], h, qt * P:(qt + 1) * P], (lambda c0, cw, u=u: K2[r[u], h, c0:c0 + cw]), s0)
                for u in range(2)]

    def diff_combine(E, st_, n):
        dve.do(V.tensor_scalar, E[0][:, 0:n], E[0][:, 0:n], st_[0][:, 2:3], None, ALU.mult)
        dve.do(V.tensor_tensor, st_[1][:, 3:4], st_[1][:, 2:3], lam[:, 5:6], ALU.mult)
        return dve.do(V.scalar_tensor_tensor, E[0][:, 0:n], E[1][:, 0:n], st_[1][:, 3:4], E[0][:, 0:n],
                      ALU.mult, ALU.add)
    attention_steps([(h, qt) for h in range(DT) for qt in range(6)], diff_parts, 64 ** -0.5, diff_combine,
                    lambda step, b: VTM[:, b, step[0] * P:(step[0] + 1) * P],
                    lambda step: O2[:, step[0], step[1] * P:(step[1] + 1) * P])
    k.fence()
    pe.wait(make_spread2())
    hn = HeadNorm(DT, "sel_all", SEG2, TB2 + 2 * T2)
    for h in range(DT):
        hn.square(h, O2[:, h, :], [])
    hn.root(P)
    pair_read = [[], [], []]
    for h in range(DT):
        pair_read[h % 3] = [hn.scale(h, O2[:, h, :], lam[:, 6:7], (2 * (h % 3), 2 * (h % 3) + 1), pair_read[h % 3])]
    k.fence()
    banks = Banks([0, 1, 2, 3, 4, 5])
    project_out(SEG2, banks)
    k.fence()
    swiglu(SEG2, mod_norm(1, SEG2))

    modulation(1)
    hm = mod_norm(0, SEG2)
    act.dma(load_c, tab[:], a["tab128"], w=[dve.done.now()])
    dve.wait(load_c.now())
    banks = Banks([0, 1, 2, 3])
    cut = Cut(A2 + 2 * 6144)
    cut_up_to(80)
    project_heads([(Q2, DT, p2("gq"), SEG1), (K2, 2, p2("gk"), SEG2)], c_("rot_ax128"), "sel_all", 128, banks, cut,
                  lambda q: hm[q])
    values_token_major(2, 256)

    def gqa_parts(step):
        h, qt = step
        return [(Q2[:, h, qt * P:(qt + 1) * P], (lambda c0, cw: K2[:, h // 4, c0:c0 + cw]), 0)]

    def gqa_combine(E, st_, n):
        return dve.do(V.tensor_scalar, E[0], E[0], st_[0][:, 2:3], None, ALU.mult)
    attention_steps([(h, qt) for h in range(DT) for qt in range(4)], gqa_parts, 128 ** -0.5, gqa_combine,
                    lambda step, b: VTM[:, b, step[0] // 4 * P:(step[0] // 4 + 1) * P],
                    lambda step: O2[:, step[0], step[1] * P:(step[1] + 1) * P])
    k.fence()
    banks = Banks([0, 1, 2, 3])
    project_out(SEG1, banks)
    k.fence()
    swiglu(SEG1, mod_norm(1, SEG1))
    spend_to_turn()
    k.fence()
    act.dma(out_d, a["out"], X[:, :, 0:S])
    act.wait(out_d.now())
    return k


def _tiles(w):
    kk, nn = w.shape
    return w.reshape(kk // P, P, nn // P, P).transpose(2, 0, 1, 3).reshape(-1, P, P)


def _rows(w, width):
    kk, nn = w.shape
    return (w.reshape(kk // P, P, nn // (width * P), width, P).transpose(2, 0, 3, 1, 4).reshape(-1, P, P))


def _inter(*ws):
    cols = [w.reshape(w.shape[0] // P, P, w.shape[1] // P, P).transpose(2, 0, 1, 3) for w in ws]
    return np.concatenate(cols, axis=1).reshape(-1, P, P)


def _feat(v):
    return v.reshape(-1, P).T


def _zeros(*shape):
    return np.zeros(shape, np.float32)


def _constants():
    con = np.zeros((P, NCONST), np.float32)

    def put(name, m):
        con[:, CONST[name]:CONST[name] + m.shape[1]] = m
    eye = np.eye(P, dtype=np.float32)
    blk = np.kron(np.eye(2), np.ones((64, 64)))
    put("ident", eye)
    put("ones_d", np.full((P, P), 1.0 / D))
    put("ones_128", np.full((P, P), 1.0 / P))
    put("blk", blk)
    put("blk_64", blk / 64)

    def rot(n, group, half):
        m = np.zeros((P, P))
        for i in range(P):
            if i % group < half:
                m[i + half, i] = -1.0
            else:
                m[i - half, i] = 1.0
        return m
    put("rot_nx", rot(P, 64, 32))
    put("rot_ax64", rot(P, 32, 16))
    put("rot_ax128", rot(P, 64, 32))
    s, t = np.meshgrid(np.arange(CH), np.arange(CH), indexing="ij")
    same = (s // 16) == (t // 16)
    two = lambda m: np.concatenate([m, m], axis=0).astype(np.float32)
    put("m_diagT", two((s < t) & same))
    put("m_offT", two((s < t) & ~same))
    put("m_diag", two((t < s) & same))
    put("m_incT", two(s <= t))
    put("m_strT", two(s < t))
    put("eye64", two(s == t))
    seg = np.ones((P, S))
    seg[:, ::CH] = 0
    put("segs", seg)
    q, kk = np.meshgrid(np.arange(P), np.arange(2 * P), indexing="ij")
    dist = q + P - kk
    put("band", np.where((dist >= 0) & (dist < P), 0.0, NEG))
    half = HD // 2
    inv = np.power(np.float32(10000.0), -np.arange(half, dtype=np.float32) / half)
    sel = np.zeros((P, 30))
    sel[:64, 14] = 1
    sel[64:, 15] = 1
    put("sel", sel)
    sel_all = np.zeros((P, 30))
    sel_all[:, 14:16] = 1
    put("sel_all", sel_all)
    put("invf", np.tile(inv, 4)[:, None])
    return con


def _axial(dh):
    half = dh // 2
    inv = np.float32(10000.0) ** (-np.arange(0, half, 2, dtype=np.float32) / np.float32(half))
    pos = np.arange(S)
    r = (pos // 64).astype(np.float32)[:, None] * inv[None]
    c = (pos % 64).astype(np.float32)[:, None] * inv[None]
    ang = np.concatenate([r, r, c, c], axis=-1).astype(np.float32)
    n = P // dh
    return np.stack([np.tile(np.cos(ang).T, (n, 1)), np.tile(np.sin(ang).T, (n, 1))], axis=1).astype(np.float32)


def layout(i):
    f = {n: np.asarray(v) for n, v in i.items()}
    ws = []
    for l in range(L):
        w = f["w_in"][l]
        c = np.cumsum([0, 1024, 256, 256, 3072, 64, 64, 160, 1024, 1024])
        q, kk, v, rkv, wd, ad, gd, ga, gb = (w[:, c[n]:c[n + 1]] for n in range(9))
        ws += [_tiles(q), _tiles(kk), _rows(v, 2), _inter(ga, f["w_o_att"][l])]
        low = np.concatenate([wd, ad, gd, _zeros(D, 96)], axis=1)
        ws.append(_tiles(low))
        used = 64 + 16 + 16 + 128 + 24
        ws.append(_zeros(-used % TURN, P, P))
        ws.append(_tiles(rkv))
        used += -used % TURN + 192
        ws.append(_tiles(np.concatenate([f["rw_w2"][l], f["rw_a2"][l]], axis=0)))
        ws.append(_tiles(np.concatenate([f["rw_g2"][l], _zeros(96, D)], axis=0)))
        ws += [_inter(gb, f["w_o_rw"][l]), _tiles(f["w_out"][l])]
        used += 8 + 16 + 128 + 64
        ws.append(_zeros(-used % TURN, P, P))
        used += -used % TURN
        ws += [_inter(f["w_up"][l][:, :FFN], f["w_up"][l][:, FFN:]), _tiles(f["w_down"][l])]
        wp, wg = f["w_ple"][l], f["w_ple_gate"][l]
        ws.append(_inter(wp, wg))
        used += 24 * FT + 80
        ws.append(_zeros(-used % TURN, P, P))
    for l in range(2):
        ws.append(_rows(f["ada_w_2"][l], 4))
        if l == 0:
            w = f["diff_w_in_2"][0]
            ws += [_tiles(w[:, :2 * D]), _rows(w[:, 2 * D:], 4), _tiles(f["diff_w_out_2"][0])]
        else:
            w = f["gqa_w_in_2"][0]
            ws += [_tiles(w[:, :D + 256]), _rows(w[:, D + 256:], 2), _tiles(f["gqa_w_out_2"][0])]
        gu = f["ffn_w_gu_2"][l]
        ws += [_inter(gu[:, :FFN], gu[:, FFN:]), _tiles(f["ffn_w_down_2"][l])]
    n = sum(w.shape[0] for w in ws)
    ws.append(_zeros(-n % TURN, P, P))
    n += -n % TURN
    stream = np.concatenate(ws, axis=0).reshape(n // PIECE, PIECE, P, P).transpose(0, 2, 1, 3)
    par1 = np.zeros((L, P, NC1), np.float32)
    par2 = np.zeros((P, NC2), np.float32)

    def put1(l, name, m):
        par1[l, :, COLS1[name]:COLS1[name] + m.shape[1]] = m

    def put2(name, m):
        par2[:, COLS2[name]:COLS2[name] + m.shape[1]] = m
    for l in range(L):
        mu = f["rw_mu"][l]
        put1(l, "pre", _feat(f["norm_mix_pre"][l]))
        put1(l, "mu_rkv", _feat(mu[:3072]))
        put1(l, "mu_low", _feat(np.concatenate([mu[3072:], _zeros(96)])))
        for n_, s_ in (("w0", "rw_w0"), ("a0", "rw_a0"), ("k_k", "rw_k_k"), ("k_a", "rw_k_a"), ("gn_w", "rw_gn_w"),
                       ("gn_b", "rw_gn_b"), ("post", "norm_mix_post"), ("fpre", "norm_ffn_pre"),
                       ("cb", "conv_b"), ("fpost", "norm_ffn_post"), ("ple", "norm_ple")):
            put1(l, n_, _feat(f[s_][l]))
        put1(l, "r_k", _feat(f["rw_r_k"][l].reshape(-1)))
        put1(l, "cw", _feat(f["conv_w"][l].reshape(-1)))
        put1(l, "sinks", np.broadcast_to(f["att_sinks"][l].reshape(4, 2, 2).transpose(0, 2, 1).reshape(1, -1), (P, NQH)))
    put2("ada_b", np.concatenate([_feat(f["ada_b_2"][l]) for l in range(2)], axis=1))
    put2("norm1", np.concatenate([_feat(f["norm1_g_2"][l]) for l in range(2)], axis=1))
    put2("norm2", np.concatenate([_feat(f["norm2_g_2"][l]) for l in range(2)], axis=1))
    put2("dq", np.tile(f["diff_q_norm_2"][0], 2)[:, None])
    put2("dk", np.tile(f["diff_k_norm_2"][0], 2)[:, None])
    put2("gq", f["gqa_q_norm_2"][0][:, None])
    put2("gk", f["gqa_k_norm_2"][0][:, None])
    put2("subln", f["diff_subln_2"][0][:, None])
    lam = np.zeros((P, 4), np.float32)
    for n_, s_ in enumerate(("q1", "q2", "k1", "k2")):
        lam[:64, n_] = f[f"diff_lambda_{s_}_2"][0]
    put2("lam", lam)
    put2("cond", np.stack([_feat(f["c_2"][0]), _feat(f["c_ctx_2"])], axis=2).reshape(P, 16))

    def fm(x):
        return np.ascontiguousarray(x.T.reshape(-1, P, x.shape[0]).transpose(1, 0, 2))
    return {
        "w": np.ascontiguousarray(stream), "con": _constants(), "par1": par1, "par2": par2,
        "pos": np.ascontiguousarray(np.broadcast_to(f["positions"], (P, S))),
        "x": fm(f["x"][0]), "ctx": fm(f["ctx_2"][0]),
        "p": np.stack([fm(f["p"][l, 0]) for l in range(L)]),
        "tab64": _axial(64), "tab128": _axial(128),
    }


def _build(arrays, per, new_bass):
    nc = new_bass()
    aps = {n: nc.dram_tensor("in_" + n, v.shape, mybir.dt.from_np(v.dtype), kind="ExternalInput").ap()
           for n, v in arrays.items()}
    aps["out"] = nc.dram_tensor("out_x", (P, DT, S), F32, kind="ExternalOutput").ap()
    k = program(nc, aps, per)
    return nc, k


def kernel(**inputs):
    import concourse.bacc as bacc
    from concourse.bass_utils import run_bass_kernel_spmd

    def new_bass():
        return bacc.Bacc("TRN2", target_bir_lowering=False, num_devices=1)

    arrays = layout(inputs)
    _, counted = _build(arrays, {}, new_bass)
    nc, k = _build(arrays, counted.counted, new_bass)
    assert k.counted == counted.counted
    r = run_bass_kernel_spmd(nc, [{"in_" + n: v for n, v in arrays.items()}], core_ids=[0])
    out = r.results[0]["out_x"]
    return np.ascontiguousarray(out.transpose(1, 0, 2).reshape(D, S).T)[None]
```
